# Optimizing a Trainium2 kernel written in Bass

```python
import jax, jax.numpy as jnp
from jax import lax
import numpy as np

D_MODEL = 2048
BATCH = 1
SEQ = 512
DEPTH = 1

CHUNK = 64
HEAD_DIM = 64
EPS = 1e-6
MASK_VALUE = -1e30

A_Q_HEADS = 16
A_KV_HEADS = 4
A_GROUP = A_Q_HEADS // A_KV_HEADS
A_WINDOW = 128
A_WINDOW_CHUNKS = A_WINDOW // CHUNK
ROPE_THETA = 500000.0
ROT_DIM = HEAD_DIM // 4

B_HEADS = 16
B_LEFT_CHUNKS = 8
B_BAND = (B_LEFT_CHUNKS + 1) * CHUNK
REL_MIN = -(CHUNK - 1)
REL_MAX = 256
N_REL = REL_MAX - REL_MIN + 1

A_Q_W = A_Q_HEADS * HEAD_DIM
A_KV_W = A_KV_HEADS * HEAD_DIM
B_W = B_HEADS * HEAD_DIM
IN_W = A_Q_W + 2 * A_KV_W + 3 * B_W + 2 * D_MODEL

PEER_HEADS = 8
PEER_KEYS = 128
PEER_EXPERTS = PEER_KEYS * PEER_KEYS
PEER_QDIM = 256
PEER_HALF = PEER_QDIM // 2
PEER_TOPK = 16
TOKEN_BLOCK = 128

kernel_name = "hybrid_swa_sink_chunkrel_peer"

def rms_norm(x, gain):
    xf = x.astype(jnp.float32)
    y = xf * lax.rsqrt(jnp.mean(xf * xf, axis=-1, keepdims=True) + EPS)
    return (y * gain.astype(jnp.float32)).astype(x.dtype)

def partial_rope(x, positions):
    half = ROT_DIM // 2
    inv_freq = ROPE_THETA ** (-jnp.arange(0, ROT_DIM, 2, dtype=jnp.float32) / ROT_DIM)
    ang = positions.astype(jnp.float32)[:, None] * inv_freq[None, :]
    cos = jnp.cos(ang)[None, :, None, :]
    sin = jnp.sin(ang)[None, :, None, :]
    xf = x.astype(jnp.float32)
    x1 = xf[..., :half]
    x2 = xf[..., half:ROT_DIM]
    rot = jnp.concatenate([x1 * cos - x2 * sin, x2 * cos + x1 * sin], axis=-1)
    return jnp.concatenate([rot.astype(x.dtype), x[..., ROT_DIM:]], axis=-1)

def sliding_window_sink_attention(q, k, v, sinks):
    b, s = q.shape[:2]
    nc = s // CHUNK
    wk = A_WINDOW_CHUNKS * CHUNK
    pad = (A_WINDOW_CHUNKS - 1) * CHUNK
    qc = q.reshape(b, nc, CHUNK, A_KV_HEADS, A_GROUP, HEAD_DIM).astype(jnp.float32)
    padw = ((0, 0), (pad, 0), (0, 0), (0, 0))
    kp = jnp.pad(k, padw).reshape(b, nc + A_WINDOW_CHUNKS - 1, CHUNK, A_KV_HEADS, HEAD_DIM)
    vp = jnp.pad(v, padw).reshape(b, nc + A_WINDOW_CHUNKS - 1, CHUNK, A_KV_HEADS, HEAD_DIM)
    kb = jnp.concatenate([kp[:, j:j + nc] for j in range(A_WINDOW_CHUNKS)], axis=2).astype(jnp.float32)
    vb = jnp.concatenate([vp[:, j:j + nc] for j in range(A_WINDOW_CHUNKS)], axis=2).astype(jnp.float32)
    scores = jnp.einsum('bnqkgd,bnskd->bnkgqs', qc, kb) * (HEAD_DIM ** -0.5)
    key_chunk = jnp.arange(nc)[:, None] + (jnp.arange(wk) // CHUNK)[None, :] - (A_WINDOW_CHUNKS - 1)
    valid = key_chunk >= 0
    scores = jnp.where(valid[None, :, None, None, None, :], scores, MASK_VALUE)
    sink = sinks.astype(jnp.float32).reshape(A_KV_HEADS, A_GROUP)[None, None, :, :, None, None]
    m = jnp.maximum(jnp.max(scores, axis=-1, keepdims=True), sink)
    p = jnp.exp(scores - m)
    probs = p / (jnp.sum(p, axis=-1, keepdims=True) + jnp.exp(sink - m))
    out = jnp.einsum('bnkgqs,bnskd->bnqkgd', probs, vb)
    return out.reshape(b, s, A_Q_W).astype(q.dtype)

def chunked_relbias_attention(q, k, v, rel_bias):
    b, s = q.shape[:2]
    nc = s // CHUNK
    pad = B_LEFT_CHUNKS * CHUNK
    padw = ((0, 0), (pad, 0), (0, 0), (0, 0))
    kp = jnp.pad(k, padw).astype(jnp.float32)
    vp = jnp.pad(v, padw).astype(jnp.float32)
    qc = q.reshape(b, nc, CHUNK, B_HEADS, HEAD_DIM).astype(jnp.float32).transpose(1, 0, 2, 3, 4)
    rel = jnp.arange(CHUNK)[:, None] - jnp.arange(B_BAND)[None, :] + pad
    rel_idx = jnp.clip(rel, REL_MIN, REL_MAX) - REL_MIN
    bias = rel_bias.astype(jnp.float32)[:, rel_idx]
    scale = HEAD_DIM ** -0.5

    def one_chunk(args):
        c, q_blk = args
        start = c * CHUNK
        k_blk = lax.dynamic_slice_in_dim(kp, start, B_BAND, axis=1)
        v_blk = lax.dynamic_slice_in_dim(vp, start, B_BAND, axis=1)
        sc = jnp.einsum('bqhd,bkhd->bhqk', q_blk, k_blk) * scale + bias[None]
        valid = (start + jnp.arange(B_BAND)) >= pad
        sc = jnp.where(valid[None, None, None, :], sc, MASK_VALUE)
        p = jax.nn.softmax(sc, axis=-1)
        return jnp.einsum('bhqk,bkhd->bqhd', p, v_blk)

    out = lax.map(one_chunk, (jnp.arange(nc), qc))
    return out.transpose(1, 0, 2, 3, 4).reshape(b, s, B_W).astype(q.dtype)

def peer_ffn(x, w_query, sub_keys1, sub_keys2, expert_down, expert_up):
    b, s, d = x.shape
    tok = x.reshape(-1, TOKEN_BLOCK, d)

    def block(xt):
        qry = (xt @ w_query).reshape(TOKEN_BLOCK, PEER_HEADS, 2, PEER_HALF).astype(jnp.float32)
        s1 = jnp.einsum('thd,hnd->thn', qry[:, :, 0], sub_keys1.astype(jnp.float32))
        s2 = jnp.einsum('thd,hnd->thn', qry[:, :, 1], sub_keys2.astype(jnp.float32))
        v1, i1 = lax.top_k(s1, PEER_TOPK)
        v2, i2 = lax.top_k(s2, PEER_TOPK)
        cand = (v1[..., :, None] + v2[..., None, :]).reshape(TOKEN_BLOCK, PEER_HEADS, PEER_TOPK * PEER_TOPK)
        cand_idx = (i1[..., :, None] * PEER_KEYS + i2[..., None, :]).reshape(TOKEN_BLOCK, PEER_HEADS, PEER_TOPK * PEER_TOPK)
        top_s, pos = lax.top_k(cand, PEER_TOPK)
        idx = jnp.take_along_axis(cand_idx, pos, axis=-1)
        gate = jax.nn.softmax(top_s, axis=-1)
        u = expert_down[idx]
        vv = expert_up[idx]
        pre = jnp.einsum('td,thkd->thk', xt, u).astype(jnp.float32)
        act = (jax.nn.gelu(pre, approximate=False) * gate).astype(xt.dtype)
        return jnp.einsum('thk,thkd->td', act, vv)

    out = lax.map(block, tok)
    return out.reshape(b, s, d)

def setup_inputs(seed: int = 0) -> dict:
    key = jax.random.key(seed)
    ks = jax.random.split(key, 20)
    f32 = jnp.float32
    nrm = lambda k, shape, sc: jax.random.normal(k, shape, f32) * sc
    L = DEPTH
    return {
        'x': nrm(ks[0], (BATCH, SEQ, D_MODEL), 1.0),
        'norm1_gain': 1.0 + nrm(ks[1], (L, D_MODEL), 0.02),
        'w_in': nrm(ks[2], (L, D_MODEL, IN_W), D_MODEL ** -0.5),
        'b_gate': nrm(ks[3], (L, 2 * D_MODEL), 0.02),
        'q_norm_a': 1.0 + nrm(ks[4], (L, HEAD_DIM), 0.02),
        'k_norm_a': 1.0 + nrm(ks[5], (L, HEAD_DIM), 0.02),
        'attn_sinks': nrm(ks[6], (L, A_Q_HEADS), 0.5),
        'q_norm_b': 1.0 + nrm(ks[7], (L, HEAD_DIM), 0.02),
        'k_norm_b': 1.0 + nrm(ks[8], (L, HEAD_DIM), 0.02),
        'rel_bias': nrm(ks[9], (L, B_HEADS, N_REL), 0.1),
        'w_branch_a': nrm(ks[10], (L, A_Q_W, D_MODEL), A_Q_W ** -0.5),
        'w_branch_b': nrm(ks[11], (L, B_W, D_MODEL), B_W ** -0.5),
        'w_out': nrm(ks[12], (L, D_MODEL, D_MODEL), D_MODEL ** -0.5),
        'norm2_gain': 1.0 + nrm(ks[13], (L, D_MODEL), 0.02),
        'peer_w_query': nrm(ks[14], (L, D_MODEL, PEER_HEADS * PEER_QDIM), D_MODEL ** -0.5),
        'peer_sub_keys1': nrm(ks[15], (L, PEER_HEADS, PEER_KEYS, PEER_HALF), PEER_HALF ** -0.5),
        'peer_sub_keys2': nrm(ks[16], (L, PEER_HEADS, PEER_KEYS, PEER_HALF), PEER_HALF ** -0.5),
        'peer_down': nrm(ks[17], (L, PEER_EXPERTS, D_MODEL), D_MODEL ** -0.5),
        'peer_up': nrm(ks[18], (L, PEER_EXPERTS, D_MODEL), PEER_HEADS ** -0.5),
    }

def reference(x, norm1_gain, w_in, b_gate, q_norm_a, k_norm_a, attn_sinks, q_norm_b, k_norm_b,
              rel_bias, w_branch_a, w_branch_b, w_out, norm2_gain, peer_w_query,
              peer_sub_keys1, peer_sub_keys2, peer_down, peer_up):
    b, s, d = x.shape
    positions = jnp.arange(s, dtype=jnp.int32)
    o1 = A_Q_W
    o2 = o1 + A_KV_W
    o3 = o2 + A_KV_W
    o4 = o3 + B_W
    o5 = o4 + B_W
    o6 = o5 + B_W
    h = x
    for l in range(DEPTH):
        xn = rms_norm(h, norm1_gain[l])
        proj = xn @ w_in[l]
        qa = proj[..., :o1].reshape(b, s, A_Q_HEADS, HEAD_DIM)
        ka = proj[..., o1:o2].reshape(b, s, A_KV_HEADS, HEAD_DIM)
        va = proj[..., o2:o3].reshape(b, s, A_KV_HEADS, HEAD_DIM)
        qb = proj[..., o3:o4].reshape(b, s, B_HEADS, HEAD_DIM)
        kb = proj[..., o4:o5].reshape(b, s, B_HEADS, HEAD_DIM)
        vb = proj[..., o5:o6].reshape(b, s, B_HEADS, HEAD_DIM)
        gates = jax.nn.sigmoid((proj[..., o6:] + b_gate[l]).astype(jnp.float32)).astype(h.dtype)
        g_a = gates[..., :D_MODEL]
        g_b = gates[..., D_MODEL:]

        qa = partial_rope(rms_norm(qa, q_norm_a[l]), positions)
        ka = partial_rope(rms_norm(ka, k_norm_a[l]), positions)
        y_a = sliding_window_sink_attention(qa, ka, va, attn_sinks[l])

        qb = rms_norm(qb, q_norm_b[l])
        kb = rms_norm(kb, k_norm_b[l])
        y_b = chunked_relbias_attention(qb, kb, vb, rel_bias[l])

        mixed = g_a * (y_a @ w_branch_a[l]) + g_b * (y_b @ w_branch_b[l])
        h = h + mixed @ w_out[l]

        hn = rms_norm(h, norm2_gain[l])
        h = h + peer_ffn(hn, peer_w_query[l], peer_sub_keys1[l], peer_sub_keys2[l],
                         peer_down[l], peer_up[l])
    return h


_drawn_inputs = setup_inputs


def setup_inputs(seed=0):
    import zlib

    import numpy as np

    out = dict(_drawn_inputs(seed))
    spreads = {}
    factors = {'norm1_gain': 4.901,
     'b_gate': 8.0,
     'q_norm_a': 8.0,
     'k_norm_a': 7.778,
     'attn_sinks': 8.0,
     'q_norm_b': 8.0,
     'k_norm_b': 8.0,
     'rel_bias': 3.658,
     'norm2_gain': 8.0}
    for name, (base, spread) in spreads.items():
        noise = np.random.default_rng([zlib.crc32(name.encode()), seed]).standard_normal(out[name].shape)
        drawn = base * np.exp(spread * noise) if base else spread * noise
        out[name] = __import__('jax').numpy.asarray(drawn.astype(out[name].dtype))
    for name, factor in factors.items():
        out[name] = (out[name] * factor).astype(out[name].dtype)
    return out
```

```python
import numpy as np
import concourse.bass as bass
from concourse import mybir
from contextlib import ExitStack

D = 2048
S = 512
P = 128
CT = D // P
TT = S // P
HD = 64
EPS = 1e-6
A_PAIRS = 8
B_PAIRS = 8
A_QW, A_KVW, B_W = 1024, 256, 1024
N_GATE = 2 * CT
HEADS = 8
TOPK = 16
KEYS = 128
EXPERT_TILES = 128
GROUPS = EXPERT_TILES // 4

B_PRE = 0
B_ATT_A = 5
B_ATT_B = B_ATT_A + 4 * 7
B_EPI = B_ATT_B + 4 * 8
B_BRANCH = B_EPI + 3
B_OUT = B_BRANCH + 16
B_QUERY = B_OUT + 16
B_DOWN = B_QUERY + 16
B_UP = B_DOWN + EXPERT_TILES
N_BLOCKS = B_UP + 4 * GROUPS

DOWN_TOPK = 10
GATE_GROUPS = 16
GT = S // GATE_GROUPS

MAIN, AUX, SC, TR, YB = 0, 2, 3, 5, 7

F32, F32R, U32 = mybir.dt.float32, mybir.dt.float32r, mybir.dt.uint32
ACT = mybir.ActivationFunctionType
ALU = mybir.AluOpType
AX = mybir.AxisListType.X

C_G1, C_G2, C_BG, C_QA, C_KA, C_QB, C_KB, C_SINK, C_EPS, N_COLS = 0, 16, 32, 64, 65, 66, 67, 68, 84, 85


def need(eng, sem, value):
    if not (isinstance(value, int) and value <= 0):
        eng.wait_ge(sem, value)


def repeat(eng, n, body, first=0):
    body(first)
    if n - first == 2:
        body(first + 1)
    elif n - first > 2:
        with eng.Fori(first + 1, n) as i:
            body(i)


def build(nc, x_t, w_stream, small, keys_t, rel_ext, consts, out):
    ctx = ExitStack()
    with ctx:
        sem = lambda name: ctx.enter_context(nc.semaphore(name))
        K = 1024
        BASE = 16512

        def at(name, kb, cols, dt=F32):
            return nc.alloc_sbuf_tensor_at(name, [P, cols], dt, offset=BASE + int(kb * K))

        raw = [at(f"w_raw{s}", 8 * s, 2048) for s in range(2)]
        whi = [at(f"w_hi{s}", 16 + 8 * s, 2048, F32R) for s in range(2)]
        wlo = [at(f"w_lo{s}", 32 + 8 * s, 2048, F32R) for s in range(2)]
        cst = at("cst", 48, 6 * 128)
        ident, head_ones, rot_t, ones = (cst[:, 128 * k:128 * k + 128] for k in range(4))
        mask_a = at("mask_a", 51, 256)
        iota = at("iota", 52, 128)
        cols = at("cols", 52.5, N_COLS)
        qscaled = at("qscaled", 52.875, 2)
        xn_hi, xn_lo = at("xn_hi", 53, CT * S, F32R), at("xn_lo", 85, CT * S, F32R)
        y_hi, y_lo = at("y_hi", 53, CT * S, F32R), at("y_lo", 85, CT * S, F32R)
        h = at("h", 53, CT * S)
        s_all = at("s_all", 85, TT * 16 * KEYS)
        gate_buf = at("gate_buf", 85, KEYS * GT)
        oh2 = [at(f"oh2_{s}", 101 + 2 * s, 512, F32R) for s in range(2)]
        oh1 = at("oh1", 105, 512)
        ghi = [at(f"ghi_{s}", 107 + 2 * s, 512, F32R) for s in range(2)]
        glo = [at(f"glo_{s}", 111 + 2 * s, 512, F32R) for s in range(2)]
        act_hi = [at(f"act_hi{s}", 85 + 8 * s, 4 * S, F32R) for s in range(2)]
        act_lo = [at(f"act_lo{s}", 101 + 8 * s, 4 * S, F32R) for s in range(2)]
        x_raw = at("x_raw", 117, CT * S)
        y_all = at("y_all", 117, CT * S)
        mix_hi, mix_lo = at("mix_hi", 117, CT * S, F32R), at("mix_lo", 149, CT * S, F32R)
        hn_hi, hn_lo = at("hn_hi", 117, CT * S, F32R), at("hn_lo", 149, CT * S, F32R)
        q_st, k_st, q_at, k_at = (at(n, 149 + 2 * k, S) for k, n in enumerate(["q_st", "k_st", "q_at", "k_at"]))
        v_raw, v_st, v_at = (at(n, 157 + 2 * k, S) for k, n in enumerate(["v_raw", "v_st", "v_at"]))
        g_raw = [at(f"g_raw{s}", 163 + 2 * s, S) for s in range(3)]
        sq, var, rst, newt = (at(n, 169 + 2 * k, S) for k, n in enumerate(["sq", "var", "rst", "newt"]))
        cos, sin = at("cos", 177, S), at("sin", 179, S)
        ka = [at(f"ka{g}", 181 + 2 * g, S) for g in range(2)]
        va = [at(f"va{g}", 185 + 2 * g, S) for g in range(2)]
        bias = [at(f"bias{s}", 189 + 2 * s, S) for s in range(2)]
        sc = [at(f"scores{s}", 193 + 2 * s, S) for s in range(2)]
        pt = [at(f"probs_t{s}", 197 + 2 * s, S) for s in range(2)]
        rope_t = at("rope_t", 201, S)
        xn_t = [at(f"xn_t{s}", 203 + 2 * s, S) for s in range(2)]
        mx, negm, psm, esk, rcp = (at(n, 207 + k / 32, 2) for k, n in enumerate(["mx", "negm", "psm", "esk", "rcp"]))
        g_in = [at(f"g_in{s}", 181 + 4 * s, 2 * S) for s in range(4)]
        m1 = [at(f"m1_{s}", 197 + 2 * s, S) for s in range(2)]
        m2 = [at(f"m2_{s}", 201 + 2 * s, S) for s in range(2)]
        ss2, sq2, var2, rst2, newt2 = (at(n, 181 + 2 * k, S) for k, n in enumerate(["ss2", "sq2", "var2", "rst2", "newt2"]))
        keys = at("keys", 191, 16 * KEYS)
        q_sb = [at(f"q_sb{s}", 199 + 2 * s, S) for s in range(2)]
        hn_t = [at(f"hn_t{s}", 203 + 2 * s, S) for s in range(2)]
        gel_all = at("gel_all", 181, 4 * S)
        gel = [gel_all[:, S * s:S * (s + 1)] for s in range(4)]
        tk_in, tk_m, cand, cand_m, eq, prod = (
            at(n, 189 + k, 256) for k, n in enumerate(["tk_in", "tk_m", "cand", "cand_m", "eq", "prod"]))
        tk_v, tk_i = at("tk_v", 195, 32), at("tk_i", 195.125, 32, U32)
        tk_if, top_v = at("tk_if", 195.25, 32), at("top_v", 195.375, 16)
        top_p, top_a, top_b = (at(n, 195.5 + k / 16, 16, U32) for k, n in enumerate(["top_p", "top_a", "top_b"]))
        top_f = at("top_f", 195.75, 32)
        i1_all, i2_all, tv_all = (at(n, 196 + 2 * k, S) for k, n in enumerate(["i1_all", "i2_all", "tv_all"]))
        tv_sum, tv_rec = at("tv_sum", 202, 32), at("tv_rec", 202.25, 32)
        i1_t, i2_t = at("i1_t", 189, S), at("i2_t", 191, S)
        gt_hi, gt_lo = at("gt_hi", 193, S), at("gt_lo", 203, S)
        gel_in = [at("gel_in0", 189, 4 * S), at("gel_in1", 117, 4 * S)]
        g_exp = [at("g_exp0", 197, 4 * S), at("g_exp1", 125, 4 * S)]

        ps = ctx.enter_context(nc.psum_tensor("ps", [P, 8, 512], F32))

        bias_skew = nc.dram_tensor("bias_skew", [16, P * 640], F32).ap()
        gate_dram = nc.dram_tensor("gate_dram", [N_GATE, P, S], F32).ap()
        gel_dram = nc.dram_tensor("gel_dram", [GROUPS, P, 4 * S], F32).ap()
        g_dram = nc.dram_tensor("g_dram", [GATE_GROUPS, P, KEYS * GT], F32).ap()

        s_x = [sem(f"x_in{k}") for k in range(4)]
        s_const = sem("consts_in")
        s_ext = sem("rel_ext_spread")
        raw_in = [sem(f"raw_in{s}") for s in range(2)]
        hi_ready, lo_ready = sem("w_hi_ready"), sem("w_lo_ready")
        quarters = sem("mm_quarters")
        sq_acc, xsq, ss_mm = sem("sq_summed"), sem("x_squared"), sem("sum_over_features")
        y0_ready = sem("rsqrt_guess")
        xs_ready, xhi_ready, xlo_ready = sem("x_scaled"), sem("x_hi_ready"), sem("x_lo_ready")
        qs_ready = sem("gains_scaled")
        tile_out = sem("tile_out")
        sq_ready, ss_ready, var_ready, nrm_done = sem("sq_ready"), sem("ss_ready"), sem("var_ready"), sem("nrm_done")
        rot_ready, rope_done = sem("rot_ready"), sem("rope_done")
        vt_ready, v_sb = sem("vt_ready"), sem("v_sb")
        g_out = [sem(f"gate_stored{s}") for s in range(3)]
        att_ready = sem("att_operands")
        s_qk, s_sm, s_exp, s_nrm = sem("scores"), sem("scores_max"), sem("exps"), sem("probs")
        s_tr, s_pt, s_pv, y_done = sem("probs_transposed"), sem("probs_t_sb"), sem("attended"), sem("y_done")
        bias_in = [sem(f"bias_in{s}") for s in range(2)]
        yhi_ready, ylo_ready = sem("y_hi_ready"), sem("y_lo_ready")
        gin = [sem(f"gate_loaded{s}") for s in range(4)]
        gb_ready, sig_ready, mix_done = sem("gate_biased"), sem("gate_sigmoid"), sem("mix_done")
        xh_in, h_done, ss2_done, ss2_mm, y02 = sem("x_again"), sem("h_done"), sem("h_squares"), sem("h_sum"), sem("h_guess")
        hs_ready, hhi_ready, hlo_ready = sem("h_scaled"), sem("hn_hi_ready"), sem("hn_lo_ready")
        keys_in, qsb_ready, ks_mm, sall = sem("keys_in"), sem("query_sb"), sem("key_scores_mm"), sem("key_scores")
        gel_done, gel_out = sem("gelu_done"), sem("gelu_stored")
        tv_sub, tv_exp, tk_done, tk_tr = sem("top_shifted"), sem("top_exp"), sem("topk_done"), sem("topk_transposed")
        gthi_ready, idx_ready = sem("gate_hi_ready"), sem("indices_ready")
        oh_ready, g_mm, g_sb, g_dma = sem("one_hots"), sem("gates_mm"), sem("gates_sb"), sem("gates_stored")
        up_in = [sem(f"up_in{s}") for s in range(2)]
        a_mul, a_hi, a_lo = sem("act_product"), sem("act_hi_ready"), sem("act_lo_ready")
        acc_done, s_out = sem("acc_done"), sem("out_stored")

        block = ctx.enter_context(nc.Block())

        def raw_count(base, j, i, per=4):
            return 16 * ((base + j) // 2 + 1) + 8 * per * i

        def skewed(head):
            return bias_skew[head, 127:127 + P * 639].rearrange("(p c) -> p c", c=639)[:, 0:512]

        @block.sync
        def _(sp):
            for k in range(4):
                sp.dma_start(x_raw[:, 2048 * k:2048 * (k + 1)], x_t[:, 2048 * k:2048 * (k + 1)]).then_inc(s_x[k], 16)

            def load(i):
                for s in range(2):
                    need(sp, hi_ready, 2 * i + s - 1)
                    need(sp, lo_ready, 2 * i + s - 1)
                    src = w_stream[s] if isinstance(i, int) else w_stream[bass.ds(2 * i + s, 1)].rearrange("a p c -> (a p) c")
                    sp.dma_start(raw[s][:, :], src).then_inc(raw_in[s], 16)

            repeat(sp, N_BLOCKS // 2, load)
            for f in range(CT):
                sp.wait_ge(acc_done, CT * (GROUPS - 1) + f + 1)
                sp.dma_start(out[:, S * f:S * (f + 1)], h[:, S * f:S * (f + 1)]).then_inc(s_out, 16)
            sp.wait_ge(s_out, 16 * CT)

        @block.gpsimd
        def _(pool):
            def split(i):
                for s in range(2):
                    pool.wait_ge(hi_ready, 2 * i + s + 1)
                    nc.gpsimd.tensor_tensor(wlo[s][:, :], raw[s][:, :], whi[s][:, :].bitcast(F32),
                                            ALU.subtract).then_inc(lo_ready, 1)
            repeat(pool, N_BLOCKS // 2, split)

        @block.scalar
        def _(act):
            def hi(base, j, i=0, per=4):
                s = (base + j) % 2
                b = base + j + per * i
                act.wait_ge(raw_in[s], raw_count(base, j, i, per))
                need(act, quarters, 4 * (b - 1))
                nc.scalar.activation(whi[s][:, :], raw[s][:, :], ACT.Copy).then_inc(hi_ready, 1)

            def take(b, s, dst):
                act.wait_ge(quarters, 4 * b + 4)
                nc.scalar.activation(dst, ps[:, MAIN + s, :], ACT.Copy).then_inc(tile_out, 1)

            def square(b, src):
                act.wait_ge(tile_out, b + 1)
                nc.scalar.activation(sq[:, :], src, ACT.Square).then_inc(sq_ready, 1)

            def rsqrt_guess(t):
                act.wait_ge(ss_ready, t + 1)
                need(act, nrm_done, t)
                nc.scalar.activation(var[:, :], ps[:, AUX, :], ACT.Identity, bias=cols[:, C_EPS:C_EPS + 1],
                                     scale=1.0 / HD)
                act.drain()
                nc.scalar.activation(rst[:, :], var[:, :], ACT.Ln)
                act.drain()
                nc.scalar.activation(rst[:, :], rst[:, :], ACT.Exp, scale=-0.5).then_inc(var_ready, 1)

            def take_v(t, dst):
                act.wait_ge(vt_ready, t + 1)
                nc.scalar.activation(dst, ps[:, AUX, :], ACT.Copy).then_inc(v_sb, 1)

            def take_gate(b, s, slot, gi, stored):
                need(act, g_out[slot], 16 * stored)
                take(b, s, g_raw[slot][:, :])
                act.wait_ge(tile_out, b + 1)
                dst = gate_dram[gi] if isinstance(gi, int) else gate_dram[bass.ds(gi, 1)].rearrange("a p c -> (a p) c")
                act.dma_start(dst, g_raw[slot][:, :]).then_inc(g_out[slot], 16)

            def keys_of(kind, s):
                return min(s % 4 + 1, 2 if kind == "A" else 4)

            def step(kind, k, a):
                if 1 <= k <= 8:
                    u = k - 1
                    n = keys_of(kind, u) * P
                    act.wait_ge(s_tr, 8 * a + u + 1)
                    if u >= 2:
                        act.wait_ge(s_pv, 8 * a + u - 1)
                    nc.scalar.activation(pt[u % 2][:, 0:n], ps[:, TR + u % 2, 0:n], ACT.Copy).then_inc(s_pt, 1)
                if k < 8:
                    n, r = keys_of(kind, k) * P, k % 2
                    act.wait_ge(s_sm, 8 * a + k + 1)
                    e = nc.scalar.activation(sc[r][:, 0:n], sc[r][:, 0:n], ACT.Exp, bias=negm[:, r:r + 1],
                                             accum_out=psm[:, r:r + 1])
                    if kind == "A":
                        c = C_SINK + 2 * a + k // 4
                        e = nc.scalar.activation(esk[:, r:r + 1], cols[:, bass.ds(c, 1)], ACT.Exp, bias=negm[:, r:r + 1])
                    e.then_inc(s_exp, 1)

            def load_bias(head, slot):
                act.dma_start(bias[slot][:, :], skewed(head)).then_inc(bias_in[slot], 16)

            act.dma_start(cst[:, 0:512], consts[:, 0:512]).then_inc(s_const, 16)
            act.dma_start(mask_a[:, :], consts[:, 512:768]).then_inc(s_const, 16)
            act.dma_start(iota[:, :], consts[:, 768:896]).then_inc(s_const, 16)
            act.dma_start(cos[:, :], consts[:, 896:1408]).then_inc(s_const, 16)
            act.dma_start(sin[:, :], consts[:, 1408:1920]).then_inc(s_const, 16)
            act.dma_start(cols[:, :], small).then_inc(s_const, 16)
            act.dma_start(bias_skew.rearrange("h (p c) -> h p c", c=640),
                          rel_ext[:, :].rearrange("h (o c) -> h o c", o=1).to_broadcast([16, P, 640])).then_inc(s_ext, 16)

            for c in range(CT):
                if c % 4 == 0:
                    act.wait_ge(s_x[c // 4], 16)
                if c >= 2:
                    act.wait_ge(sq_acc, c - 1)
                nc.scalar.activation(xn_t[c % 2][:, :], x_raw[:, S * c:S * (c + 1)], ACT.Square).then_inc(xsq, 1)
            hi(B_PRE, 0)
            act.wait_ge(s_const, 96)
            act.wait_ge(ss_mm, 1)
            nc.scalar.activation(var[:, :], ps[:, AUX, :], ACT.Identity, bias=cols[:, C_EPS:C_EPS + 1], scale=1.0 / D)
            act.drain()
            nc.scalar.activation(rst[:, :], var[:, :], ACT.Ln)
            act.drain()
            nc.scalar.activation(rst[:, :], rst[:, :], ACT.Exp, scale=-0.5).then_inc(y0_ready, 1)
            for c in range(CT):
                act.wait_ge(xs_ready, c + 1)
                nc.scalar.activation(xn_hi[:, S * c:S * (c + 1)], xn_t[c % 2][:, :], ACT.Copy,
                                     scale=cols[:, C_G1 + c:C_G1 + c + 1]).then_inc(xhi_ready, 1)
            hi(B_PRE, 1)

            take(0, 0, k_st[:, :])
            hi(B_PRE, 2)
            square(0, k_st[:, :])
            rsqrt_guess(0)
            take(1, 1, q_at[:, :])
            hi(B_PRE, 3)
            square(1, q_at[:, :])
            rsqrt_guess(1)
            take(2, 0, v_raw[:, :])
            hi(B_PRE, 4)
            take_v(0, va[0][:, :])
            take(3, 1, v_raw[:, :])
            hi(B_ATT_A, 0)
            take_v(1, va[1][:, :])
            take(4, 0, q_st[:, :])
            square(4, q_st[:, :])
            rsqrt_guess(2)

            def pair_a(i, n0):
                n, a = n0 + i, n0 - 1 + i
                b0 = B_ATT_A + 4 * (n0 - 1)
                b = b0 + 4 * i
                if not (isinstance(n, int) and n == 1):
                    take_gate(b - 1, 0, 2, 3 * n - 4, n - 2)
                hi(b0, 1, i)
                step("A", 0, a)
                step("A", 1, a)
                act.wait_ge(att_ready, a + 1)
                take(b, 1, q_st[:, :])
                hi(b0, 2, i)
                square(b, q_st[:, :])
                step("A", 2, a)
                step("A", 3, a)
                rsqrt_guess(2 + n)
                step("A", 4, a)
                take_gate(b + 1, 0, 0, 3 * n - 3, n - 1)
                hi(b0, 3, i)
                for k in (5, 6, 7):
                    step("A", k, a)
                take_gate(b + 2, 1, 1, 3 * n - 2, n - 1)
                hi(b0, 4, i)
                step("A", 8, a)
                step("A", 9, a)

            pair_a(0, 1)
            pair_a(0, 2)
            with act.Fori(0, 5) as i:
                pair_a(i, 3)

            def pair_b(i, n0, kind):
                n, a = n0 + i, n0 - 1 + i
                b0 = B_ATT_B + 4 * (n0 - 8)
                b = b0 + 4 * i
                if kind == "A":
                    take_gate(b - 1, 0, 2, 20, 6)
                else:
                    take_gate(b - 1, 0, 0, 12 + n, n - 2)
                hi(b0, 1, i)
                step(kind, 0, a)
                if kind == "B":
                    load_bias(2 * (a - 8) + 1, 1)
                step(kind, 1, a)
                act.wait_ge(att_ready, a + 1)
                take(b, 1, q_st[:, :])
                hi(b0, 2, i)
                square(b, q_st[:, :])
                step(kind, 2, a)
                step(kind, 3, a)
                rsqrt_guess(10 + 2 * (n - 8))
                step(kind, 4, a)
                take(b + 1, 0, k_st[:, :])
                hi(b0, 3, i)
                square(b + 1, k_st[:, :])
                step(kind, 5, a)
                if kind == "A":
                    act.wait_ge(s_ext, 16)
                load_bias(2 * (a - 7), 0)
                step(kind, 6, a)
                rsqrt_guess(11 + 2 * (n - 8))
                step(kind, 7, a)
                take(b + 2, 1, v_raw[:, :])
                hi(b0, 4, i)
                step(kind, 8, a)
                take_v(2 + n - 8, v_st[:, :])
                step(kind, 9, a)

            pair_b(0, 8, "A")
            with act.Fori(0, 7) as i:
                pair_b(i, 9, "B")

            take_gate(B_EPI - 1, 0, 0, 28, 14)
            hi(B_EPI, 1)
            load_bias(15, 1)
            for k in (0, 1, 2, 3):
                step("B", k, 15)
            take_gate(B_EPI, 1, 0, 29, 15)
            hi(B_EPI, 2)
            for k in (4, 5, 6):
                step("B", k, 15)
            take_gate(B_EPI + 1, 0, 1, 30, 7)
            hi(B_EPI, 3)
            for k in (7, 8, 9):
                step("B", k, 15)
            take_gate(B_EPI + 2, 1, 2, 31, 7)
            hi(B_BRANCH, 1)

            act.wait_ge(y_done, 16)
            act.wait_ge(quarters, 4 * B_BRANCH)
            for c in range(4):
                nc.scalar.activation(y_hi[:, 2048 * c:2048 * (c + 1)], y_all[:, 2048 * c:2048 * (c + 1)],
                                     ACT.Copy).then_inc(yhi_ready, 1)
            for slot, count in ((0, 16), (1, 8), (2, 8)):
                act.wait_ge(g_out[slot], 16 * count)

            def branches(i):
                act.wait_ge(ylo_ready, 4)
                need(act, mix_done, 4 * i)
                for f in range(4):
                    act.dma_start(g_in[f][:, :].rearrange("p (g t) -> p g t", g=2),
                                  gate_dram[bass.ds(8 * i + 2 * f, 2)].rearrange("g p t -> p g t")).then_inc(gin[f], 16)
                for f in range(4):
                    hi(B_BRANCH, f + 2, i)
                    act.wait_ge(gb_ready, 4 * i + f + 1)
                    nc.scalar.activation(g_in[f][:, :], g_in[f][:, :], ACT.Sigmoid).then_inc(sig_ready, 1)

            repeat(act, 4, branches)

            act.wait_ge(quarters, 4 * B_OUT)
            act.dma_start(h[:, :], x_t).then_inc(xh_in, 16)
            act.wait_ge(mix_done, 16)
            act.dma_start(keys[:, :], keys_t).then_inc(keys_in, 16)

            def project_out(i):
                for f in range(4):
                    hi(B_OUT, f + 2, i)

            repeat(act, 4, project_out)

            act.wait_ge(ss2_mm, 1)
            nc.scalar.activation(var2[:, :], ps[:, AUX, :], ACT.Identity, bias=cols[:, C_EPS:C_EPS + 1], scale=1.0 / D)
            act.drain()
            nc.scalar.activation(rst2[:, :], var2[:, :], ACT.Ln)
            act.drain()
            nc.scalar.activation(rst2[:, :], rst2[:, :], ACT.Exp, scale=-0.5).then_inc(y02, 1)
            for c in range(CT):
                act.wait_ge(hs_ready, c + 1)
                nc.scalar.activation(hn_hi[:, S * c:S * (c + 1)], hn_t[c % 2][:, :], ACT.Copy,
                                     scale=cols[:, C_G2 + c:C_G2 + c + 1]).then_inc(hhi_ready, 1)

            def queries(i):
                for f in range(4):
                    t = 4 * i + f
                    act.wait_ge(quarters, 4 * (B_QUERY + t) + 4)
                    need(act, ks_mm, t - 1)
                    nc.scalar.activation(q_sb[f % 2][:, :], ps[:, MAIN + f % 2, :], ACT.Copy).then_inc(qsb_ready, 1)
                    hi(B_QUERY, f + 2, i)

            repeat(act, 4, queries)

            def gelus(i, extra=None):
                for e in range(4):
                    t = 4 * i + e
                    act.wait_ge(quarters, 4 * (B_DOWN + t) + 4)
                    if e == 0:
                        need(act, gel_out, 16 * i)
                    nc.scalar.activation(gel[e], ps[:, MAIN + e % 2, :], ACT.Gelu).then_inc(gel_done, 1)
                    hi(B_DOWN, e + 2, i)
                    if extra:
                        extra(2 * e)
                        extra(2 * e + 1)
                act.wait_ge(gel_done, 4 * i + 4)
                dst = gel_dram[i] if isinstance(i, int) else gel_dram[bass.ds(i, 1)].rearrange("a p c -> (a p) c")
                act.dma_start(dst, gel_all[:, :]).then_inc(gel_out, 16)

            repeat(act, DOWN_TOPK, gelus)
            act.wait_ge(tv_sub, 1)
            nc.scalar.activation(tv_all[:, :], tv_all[:, :], ACT.Exp).then_inc(tv_exp, 1)
            act.wait_ge(tk_tr, 1)
            nc.scalar.activation(gt_hi[:, :].bitcast(F32R), ps[:, TR, :], ACT.Copy).then_inc(gthi_ready, 1)

            def gelus_and_gates(i):
                g = i - DOWN_TOPK

                def gates_out(q):
                    act.wait_ge(g_mm, 8 * g + q + 1)
                    if q == 0:
                        need(act, g_dma, 16 * g)
                    nc.scalar.activation(
                        gate_buf[:, :].rearrange("p (k t) -> p t k", t=GT)[:, 4 * q:4 * q + 4, :],
                        ps[:, SC + q % 2, :].rearrange("p (t k) -> p t k", t=4), ACT.Copy).then_inc(g_sb, 1)

                gelus(i, gates_out)
                act.wait_ge(g_sb, 8 * g + 8)
                dst = g_dram[g] if isinstance(g, int) else g_dram[bass.ds(g, 1)].rearrange("a p c -> (a p) c")
                act.dma_start(dst, gate_buf[:, :]).then_inc(g_dma, 16)

            repeat(act, DOWN_TOPK + GATE_GROUPS, gelus_and_gates, DOWN_TOPK)

            g_view = g_dram.rearrange("g p (k c) -> p g k c", c=4 * GT)

            def load_group(g, s):
                dst = gel_dram[g] if isinstance(g, int) else gel_dram[bass.ds(g, 1)].rearrange("a p c -> (a p) c")
                act.dma_start(gel_in[s][:, :], dst).then_inc(up_in[s], 16)
                act.dma_start(g_exp[s][:, :].rearrange("p (g c) -> p g c", g=GATE_GROUPS),
                              g_view[:, :, bass.ds(g, 1), :].rearrange("p g k c -> p (g k) c")).then_inc(up_in[s], 16)

            def act_high(n, s, e):
                act.wait_ge(a_mul, n + 1)
                nc.scalar.activation(act_hi[s][:, S * e:S * (e + 1)], gel_in[s][:, S * e:S * (e + 1)],
                                     ACT.Copy).then_inc(a_hi, 1)

            act.wait_ge(g_dma, 16 * GATE_GROUPS)
            act.wait_ge(idx_ready, 2)
            load_group(0, 0)
            with act.Fori(DOWN_TOPK + GATE_GROUPS, GROUPS) as i:
                gelus(i)
            for e in range(4):
                act_high(e, 0, e)
            act.wait_ge(quarters, 4 * B_UP)
            act.wait_ge(gel_out, 16 * GROUPS)
            load_group(1, 1)

            def up(i, last=False):
                for gg in range(2):
                    g = 2 * i + gg
                    for q in range(4):
                        if not (last and gg == 1 and q >= 2):
                            hi(B_UP, 4 * gg + q + 2, i, 8)
                        if last and gg == 1:
                            continue
                        act_high(4 * g + 4 + q, 1 - gg, q)
                    if not last:
                        act.wait_ge(a_lo, 4 * g + 4)
                        load_group(g + 2, gg)

            up(0)
            with act.Fori(1, GROUPS // 2 - 1) as i:
                up(i)
            up(GROUPS // 2 - 1, last=True)

        @block.vector
        def _(v):
            vec = nc.vector

            def newton(var_, rst_, newt_):
                vec.tensor_tensor(newt_[:, :], rst_[:, :], rst_[:, :], ALU.mult)
                v.drain()
                vec.tensor_tensor(newt_[:, :], newt_[:, :], var_[:, :], ALU.mult)
                v.drain()
                vec.tensor_scalar(newt_[:, :], newt_[:, :], -0.5, 1.5, ALU.mult, ALU.add)
                v.drain()

            def normed(t, dst, gain):
                v.wait_ge(var_ready, t + 1)
                newton(var, rst, newt)
                vec.scalar_tensor_tensor(out=dst, in0=dst, scalar=gain, in1=rst[:, :], op0=ALU.mult, op1=ALU.mult)
                v.drain()
                vec.tensor_tensor(dst, dst, newt[:, :], ALU.mult).then_inc(nrm_done, 1)

            def rope(t, src, dst):
                v.wait_ge(rot_ready, t + 1)
                vec.tensor_tensor(rope_t[:, :], ps[:, AUX, :], sin[:, :], ALU.mult)
                vec.tensor_tensor(dst, src, cos[:, :], ALU.mult)
                v.drain()
                vec.tensor_tensor(dst, dst, rope_t[:, :], ALU.add).then_inc(rope_done, 1)

            for c in range(CT):
                v.wait_ge(xsq, c + 1)
                if c == 0:
                    vec.tensor_copy(sq[:, :], xn_t[0][:, :]).then_inc(sq_acc, 1)
                else:
                    vec.tensor_tensor(sq[:, :], sq[:, :], xn_t[c % 2][:, :], ALU.add).then_inc(sq_acc, 1)
                v.drain()
            v.wait_ge(s_const, 96)
            for k, c in enumerate((C_QA, C_QB)):
                vec.tensor_scalar(qscaled[:, k:k + 1], cols[:, c:c + 1], HD ** -0.5, None, ALU.mult).then_inc(qs_ready, 1)
            v.wait_ge(y0_ready, 1)
            newton(var, rst, newt)
            vec.tensor_tensor(rst[:, :], rst[:, :], newt[:, :], ALU.mult)
            v.drain()

            def split_x(c):
                v.wait_ge(xhi_ready, c + 1)
                vec.scalar_tensor_tensor(out=xn_lo[:, S * c:S * (c + 1)], in0=xn_t[c % 2][:, :],
                                         scalar=cols[:, C_G1 + c:C_G1 + c + 1],
                                         in1=xn_hi[:, S * c:S * (c + 1)].bitcast(F32), op0=ALU.mult,
                                         op1=ALU.subtract).then_inc(xlo_ready, 1)

            for c in range(CT):
                if c >= 2:
                    v.drain()
                vec.tensor_tensor(xn_t[c % 2][:, :], x_raw[:, S * c:S * (c + 1)], rst[:, :], ALU.mult).then_inc(xs_ready, 1)
                if c >= 1:
                    split_x(c - 1)
            split_x(CT - 1)

            v.drain()
            normed(0, k_st[:, :], cols[:, C_KA:C_KA + 1])
            rope(0, k_st[:, :], ka[0][:, :])
            normed(1, q_at[:, :], cols[:, C_KA:C_KA + 1])
            rope(1, q_at[:, :], ka[1][:, :])
            normed(2, q_st[:, :], qscaled[:, 0:1])
            rope(2, q_st[:, :], q_st[:, :])

            def step(kind, k, a):
                if k >= 8:
                    return
                n, r = min(k % 4 + 1, 2 if kind == "A" else 4) * P, k % 2
                if k >= 2:
                    v.wait_ge(s_tr, 8 * a + k - 1)
                if kind == "B" and k % 4 == 0:
                    v.wait_ge(bias_in[k // 4], 16 * (a - 7))
                    tail = bias[k // 4][:, 512 - P:512]
                    vec.tensor_tensor(tail, tail, mask_a[:, P:2 * P], ALU.add)
                    v.drain()
                v.wait_ge(s_qk, 8 * a + k + 1)
                b = mask_a[:, 256 - n:256] if kind == "A" else bias[k // 4][:, 512 - n:512]
                vec.tensor_tensor(sc[r][:, 0:n], ps[:, SC + r, 0:n], b, ALU.add)
                v.drain()
                vec.reduce_max(mx[:, r:r + 1], sc[r][:, 0:n], AX)
                v.drain()
                if kind == "A":
                    c = C_SINK + 2 * a + k // 4
                    vec.tensor_scalar(negm[:, r:r + 1], mx[:, r:r + 1], cols[:, bass.ds(c, 1)], -1.0,
                                      ALU.max, ALU.mult).then_inc(s_sm, 1)
                else:
                    vec.tensor_scalar(negm[:, r:r + 1], mx[:, r:r + 1], -1.0, None, ALU.mult).then_inc(s_sm, 1)
                v.wait_ge(s_exp, 8 * a + k + 1)
                if kind == "A":
                    vec.tensor_tensor(psm[:, r:r + 1], psm[:, r:r + 1], esk[:, r:r + 1], ALU.add)
                    v.drain()
                vec.reciprocal(rcp[:, r:r + 1], psm[:, r:r + 1])
                v.drain()
                vec.tensor_scalar(sc[r][:, 0:n], sc[r][:, 0:n], rcp[:, r:r + 1], None, ALU.mult).then_inc(s_nrm, 1)

            def attended(a):
                v.wait_ge(s_pv, 8 * a + 8)
                vec.tensor_scalar(y_all[:, bass.ds(S * a, S)], ps[:, YB, :], 1.0, None, ALU.mult).then_inc(y_done, 1)

            def pair_a(i, n0):
                n, a = n0 + i, n0 - 1 + i
                v.drain()
                vec.tensor_copy(q_at[:, :], q_st[:, :]).then_inc(att_ready, 1)
                for k in range(5):
                    step("A", k, a)
                normed(2 + n, q_st[:, :], qscaled[:, 0:1])
                for k in (5, 6, 7):
                    step("A", k, a)
                rope(2 + n, q_st[:, :], q_st[:, :])
                attended(a)

            with v.Fori(0, 4) as i:
                pair_a(i, 1)
            with v.Fori(0, 3) as i:
                pair_a(i, 5)

            def pair_b(i, n0, kind):
                n, a = n0 + i, n0 - 1 + i
                v.drain()
                if kind == "B":
                    vec.tensor_copy(k_at[:, :], k_st[:, :])
                    v.wait_ge(v_sb, 2 + a - 7)
                    vec.tensor_copy(v_at[:, :], v_st[:, :])
                vec.tensor_copy(q_at[:, :], q_st[:, :]).then_inc(att_ready, 1)
                for k in range(5):
                    step(kind, k, a)
                normed(10 + 2 * (n - 8), q_st[:, :], qscaled[:, 1:2])
                for k in (5, 6, 7):
                    step(kind, k, a)
                v.drain()
                normed(11 + 2 * (n - 8), k_st[:, :], cols[:, C_KB:C_KB + 1])
                attended(a)

            pair_b(0, 8, "A")
            with v.Fori(0, 7) as i:
                pair_b(i, 9, "B")
            v.drain()
            vec.tensor_copy(k_at[:, :], k_st[:, :])
            v.wait_ge(v_sb, 10)
            vec.tensor_copy(v_at[:, :], v_st[:, :])
            vec.tensor_copy(q_at[:, :], q_st[:, :]).then_inc(att_ready, 1)
            for k in range(8):
                step("B", k, 15)
            attended(15)

            v.drain()
            for c in range(4):
                v.wait_ge(yhi_ready, c + 1)
                vec.tensor_tensor(y_lo[:, 2048 * c:2048 * (c + 1)], y_all[:, 2048 * c:2048 * (c + 1)],
                                  y_hi[:, 2048 * c:2048 * (c + 1)].bitcast(F32), ALU.subtract).then_inc(ylo_ready, 1)
            v.drain()

            def branches(i):
                for f in range(4):
                    v.wait_ge(gin[f], 16 * i + 16)
                    for g in range(2):
                        c = C_BG + 8 * i + 2 * f + g
                        e = vec.tensor_scalar(g_in[f][:, S * g:S * (g + 1)], g_in[f][:, S * g:S * (g + 1)],
                                              cols[:, bass.ds(c, 1)], None, ALU.add)
                    e.then_inc(gb_ready, 1)
                for f in range(4):
                    t = 4 * i + f
                    r = f % 2
                    bank = 4 * (f // 2) + r
                    v.wait_ge(sig_ready, t + 1)
                    v.wait_ge(quarters, 4 * (B_BRANCH + 4 * i + 2 * (f // 2) + 1) + 2 * r + 2)
                    vec.tensor_tensor(m1[r][:, :], ps[:, bank, :], g_in[f][:, 0:S], ALU.mult)
                    vec.tensor_tensor(m2[r][:, :], ps[:, bank + 2, :], g_in[f][:, S:2 * S], ALU.mult)
                    v.drain()
                    vec.tensor_tensor(m1[r][:, :], m1[r][:, :], m2[r][:, :], ALU.add)
                    v.drain()
                    vec.tensor_scalar(mix_hi[:, bass.ds(S * t, S)], m1[r][:, :], 1.0, None, ALU.mult)
                    v.drain()
                    vec.tensor_tensor(mix_lo[:, bass.ds(S * t, S)], m1[r][:, :],
                                      mix_hi[:, bass.ds(S * t, S)].bitcast(F32), ALU.subtract).then_inc(mix_done, 1)
                v.drain()

            repeat(v, 4, branches)

            vec.memset(ss2[:, :], 0.0)
            v.wait_ge(xh_in, 16)

            def project_out(i):
                for f in range(4):
                    t = 4 * i + f
                    hf = h[:, bass.ds(S * t, S)]
                    v.drain()
                    v.wait_ge(quarters, 4 * (B_OUT + t) + 4)
                    vec.tensor_tensor(hf, ps[:, MAIN + f % 2, :], hf, ALU.add).then_inc(h_done, 1)
                    v.drain()
                    vec.tensor_tensor(sq2[:, :], hf, hf, ALU.mult)
                    v.drain()
                    vec.tensor_tensor(ss2[:, :], ss2[:, :], sq2[:, :], ALU.add).then_inc(ss2_done, 1)

            repeat(v, 4, project_out)

            v.wait_ge(y02, 1)
            newton(var2, rst2, newt2)
            vec.tensor_tensor(rst2[:, :], rst2[:, :], newt2[:, :], ALU.mult)
            v.drain()

            def split_h(c):
                v.wait_ge(hhi_ready, c + 1)
                vec.scalar_tensor_tensor(out=hn_lo[:, S * c:S * (c + 1)], in0=hn_t[c % 2][:, :],
                                         scalar=cols[:, C_G2 + c:C_G2 + c + 1],
                                         in1=hn_hi[:, S * c:S * (c + 1)].bitcast(F32), op0=ALU.mult,
                                         op1=ALU.subtract).then_inc(hlo_ready, 1)

            for c in range(CT):
                if c >= 2:
                    v.drain()
                vec.tensor_tensor(hn_t[c % 2][:, :], h[:, S * c:S * (c + 1)], rst2[:, :], ALU.mult).then_inc(hs_ready, 1)
                if c >= 1:
                    split_h(c - 1)
            split_h(CT - 1)

            s_view = s_all[:, :].rearrange("p (i c) -> p i c", i=TT)

            def queries(i):
                for f in range(4):
                    t = 4 * i + f
                    v.wait_ge(ks_mm, t + 1)
                    vec.tensor_scalar(s_view[:, :, bass.ds(KEYS * t, KEYS)],
                                      ps[:, SC + f % 2, :].rearrange("p (i c) -> p i c", i=TT), 1.0, None,
                                      ALU.mult).then_inc(sall, 1)

            repeat(v, 4, queries)
            v.drain()

            def top16(src, spare, vals, idx):
                for s_, sp_, v_, i_ in zip(src, spare, vals, idx):
                    vec.max(v_[:, 0:8], s_)
                v.drain()
                for s_, sp_, v_, i_ in zip(src, spare, vals, idx):
                    vec.max_index(i_[:, 0:8], v_[:, 0:8], s_)
                    vec.match_replace(sp_, v_[:, 0:8], s_, -3.0e38)
                v.drain()
                for s_, sp_, v_, i_ in zip(src, spare, vals, idx):
                    vec.max(v_[:, 8:16], sp_)
                v.drain()
                for s_, sp_, v_, i_ in zip(src, spare, vals, idx):
                    vec.max_index(i_[:, 8:16], v_[:, 8:16], sp_)
                v.drain()

            def spread(a, n):
                return a.rearrange("p (k o) -> p k o", o=1).to_broadcast([P, TOPK, n])

            def tiled(a, n):
                return a.rearrange("p (o k) -> p o k", o=1).to_broadcast([P, n, TOPK])

            grid = lambda t: t[:, :].rearrange("p (a b) -> p a b", a=TOPK)
            with v.Fori(0, TT * HEADS) as u:
                vec.tensor_scalar(tk_in[:, :], s_all[:, bass.ds(2 * KEYS * u, 2 * KEYS)], 1.0, None, ALU.mult)
                v.drain()
                top16([tk_in[:, 0:128], tk_in[:, 128:256]], [tk_m[:, 0:128], tk_m[:, 128:256]],
                      [tk_v[:, 0:16], tk_v[:, 16:32]], [tk_i[:, 0:16], tk_i[:, 16:32]])
                vec.tensor_copy(tk_if[:, :], tk_i[:, :])
                vec.tensor_tensor(grid(cand), spread(tk_v[:, 0:16], TOPK), tiled(tk_v[:, 16:32], TOPK), ALU.add)
                v.drain()
                top16([cand[:, :]], [cand_m[:, :]], [top_v[:, :]], [top_p[:, :]])
                vec.tensor_scalar(tv_all[:, bass.ds(TOPK * u, TOPK)], top_v[:, :], 1.0, None, ALU.mult)
                vec.tensor_single_scalar(top_a[:, :], top_p[:, :], 4, ALU.logical_shift_right)
                vec.tensor_single_scalar(top_b[:, :], top_p[:, :], 15, ALU.bitwise_and)
                v.drain()
                vec.tensor_copy(top_f[:, 0:16], top_a[:, :])
                vec.tensor_copy(top_f[:, 16:32], top_b[:, :])
                v.drain()
                for half, dst in ((0, i1_all), (1, i2_all)):
                    r = slice(16 * half, 16 * half + 16)
                    vec.tensor_tensor(grid(eq), spread(top_f[:, r], TOPK), tiled(iota[:, 0:TOPK], TOPK), ALU.is_equal)
                    v.drain()
                    vec.tensor_tensor(grid(prod), grid(eq), tiled(tk_if[:, r], TOPK), ALU.mult)
                    v.drain()
                    vec.reduce_sum(dst[:, bass.ds(TOPK * u, TOPK)], grid(prod), AX)
                v.drain()

            per_head = lambda t: t[:, :].rearrange("p (u k) -> p u k", k=TOPK)
            one_each = lambda t: t[:, :].rearrange("p (u o) -> p u o", o=1).to_broadcast([P, TT * HEADS, TOPK])
            vec.tensor_copy(tv_sum[:, :], per_head(tv_all)[:, :, 0])
            v.drain()
            vec.tensor_tensor(per_head(tv_all), per_head(tv_all), one_each(tv_sum), ALU.subtract).then_inc(tv_sub, 1)
            v.wait_ge(tv_exp, 1)
            vec.reduce_sum(tv_sum[:, :], per_head(tv_all), AX)
            v.drain()
            vec.reciprocal(tv_rec[:, :], tv_sum[:, :])
            v.drain()
            vec.tensor_tensor(per_head(tv_all), per_head(tv_all), one_each(tv_rec), ALU.mult).then_inc(tk_done, 1)
            v.wait_ge(tk_tr, 3)
            vec.tensor_copy(i1_t[:, :], ps[:, TR + 1, :])
            vec.tensor_copy(i2_t[:, :], ps[:, YB, :])
            v.wait_ge(gthi_ready, 1)
            vec.tensor_tensor(gt_lo[:, :], ps[:, TR, :], gt_hi[:, :], ALU.subtract).then_inc(idx_ready, 1)
            v.drain()

            quad = lambda t: t[:, :].rearrange("p (t k) -> p t k", t=4)

            def one_hots(g):
                for q in range(8):
                    n, r = 8 * g + q, q % 2
                    four = lambda t: t[:, bass.ds(4 * n, 4)].rearrange("p (t o) -> p t o", o=1).to_broadcast([P, 4, KEYS])
                    line = iota[:, :].rearrange("p (o k) -> p o k", o=1).to_broadcast([P, 4, KEYS])
                    need(v, g_mm, n - 1)
                    vec.tensor_tensor(quad(oh2[r]), line, four(i2_t), ALU.is_equal)
                    vec.tensor_tensor(quad(oh1), line, four(i1_t), ALU.is_equal)
                    v.drain()
                    vec.tensor_tensor(quad(ghi[r]), quad(oh1), four(gt_hi), ALU.mult)
                    vec.tensor_tensor(quad(glo[r]), quad(oh1), four(gt_lo), ALU.mult).then_inc(oh_ready, 1)
                    v.drain()

            repeat(v, GATE_GROUPS, one_hots)
            v.wait_ge(g_mm, 8 * GATE_GROUPS)
            vec.memset(tv_sum[:, :], 0.0).then_inc(idx_ready, 1)

            def product(n, s, e):
                vec.tensor_tensor(gel_in[s][:, S * e:S * (e + 1)].rearrange("p (g t) -> p g t", g=GATE_GROUPS),
                                  gel_in[s][:, S * e:S * (e + 1)].rearrange("p (g t) -> p g t", g=GATE_GROUPS),
                                  g_exp[s][:, :].rearrange("p (g k t) -> p g k t", k=4, t=GT)[:, :, e, :],
                                  ALU.mult).then_inc(a_mul, 1)

            def low(n, s, e):
                v.wait_ge(a_hi, n + 1)
                vec.tensor_tensor(act_lo[s][:, S * e:S * (e + 1)], gel_in[s][:, S * e:S * (e + 1)],
                                  act_hi[s][:, S * e:S * (e + 1)].bitcast(F32), ALU.subtract).then_inc(a_lo, 1)

            v.wait_ge(up_in[0], 32)
            for e in range(4):
                product(e, 0, e)
            for e in range(4):
                low(e, 0, e)

            def up(i, last=False):
                for gg in range(2):
                    g = 2 * i + gg
                    for t in range(CT):
                        tile = CT * g + t
                        more = not (last and gg == 1)
                        if t == 0 and more:
                            v.wait_ge(up_in[1 - gg], 32 * i + 32 if gg == 0 else 32 * i + 64)
                            for e in range(4):
                                product(4 * g + 4 + e, 1 - gg, e)
                        v.wait_ge(quarters, 4 * B_UP + tile + 1)
                        ht = h[:, S * t:S * (t + 1)]
                        vec.tensor_tensor(ht, ps[:, t % 8, :], ht, ALU.add).then_inc(acc_done, 1)
                        if t in (1, 3, 5, 7) and more:
                            low(4 * g + 4 + t // 2, 1 - gg, t // 2)
                    v.drain()

            up(0)
            with v.Fori(1, GROUPS // 2 - 1) as i:
                up(i)
            up(GROUPS // 2 - 1, last=True)

        @block.tensor
        def _(pe):
            mm = nc.tensor.matmul

            def stream(b, s, tiles, extras=None, before=None):
                pe.wait_ge(lo_ready, b + 1)
                extras = extras or {}
                n = 0
                per = 16 // len(tiles)
                for k, (bank, free, rhs) in enumerate(tiles):
                    if free:
                        need(pe, *free)
                    for c in range(per):
                        if before:
                            pe.wait_ge(before[0], before[1] + c)
                        w = slice(P * (per * k + c), P * (per * k + c + 1))
                        hi_, lo_ = rhs[c]
                        for lhs, r in ((whi[s], hi_), (whi[s], lo_), (wlo[s], hi_)):
                            m = mm(ps[:, bank, :], lhs[:, w], r, start=(n % (3 * per) == 0),
                                   stop=(n % (3 * per) == 3 * per - 1))
                            n += 1
                            if n % 12 == 0:
                                m.then_inc(quarters, 1)
                            for work in extras.get(n, ()):
                                work()

            def operand(hi_t, lo_t, c0=0, n=CT):
                return [(hi_t[:, S * c:S * (c + 1)], lo_t[:, S * c:S * (c + 1)]) for c in range(c0, c0 + n)]

            def sum_heads(t, waits=()):
                for w in waits:
                    need(pe, *w)
                pe.wait_ge(sq_ready, t + 1)
                mm(ps[:, AUX, :], head_ones, sq[:, :], start=True, stop=True).then_inc(ss_ready, 1)

            def rotate(t, norm, src):
                pe.wait_ge(nrm_done, norm + 1)
                mm(ps[:, AUX, :], rot_t, src, start=True, stop=True).then_inc(rot_ready, 1)

            def turn_v(t, b, waits=()):
                for w in waits:
                    need(pe, *w)
                pe.wait_ge(tile_out, b + 1)
                for i in range(TT):
                    m = nc.tensor.transpose(ps[:, AUX, P * i:P * (i + 1)], v_raw[:, P * i:P * (i + 1)], ident)
                m.then_inc(vt_ready, 1)

            xn = operand(xn_hi, xn_lo)

            def proj(b, s, extras=None, before=None):
                stream(b, s, [(MAIN + s, (tile_out, b - 1), xn)], extras, before)

            pe.wait_ge(s_const, 96)
            pe.wait_ge(sq_acc, CT)
            mm(ps[:, AUX, :], ones, sq[:, :], start=True, stop=True).then_inc(ss_mm, 1)
            proj(0, 0, before=(xlo_ready, 1))
            proj(1, 1, {24: [lambda: sum_heads(0)]})
            proj(2, 0, {18: [lambda: rotate(0, 0, k_st[:, :])],
                        36: [lambda: sum_heads(1, [(rope_done, 1)])]})
            proj(3, 1, {12: [lambda: rotate(1, 1, q_at[:, :])],
                        30: [lambda: turn_v(0, 2, [(rope_done, 2)])]})
            proj(4, 0, {24: [lambda: turn_v(1, 3, [(v_sb, 1)])]})
            sum_heads(2, [(v_sb, 2)])
            rotate(2, 2, q_st[:, :])

            def step(kind, G, k, a):
                kk, vv = (ka[G], va[G]) if kind == "A" else (k_at, v_at)

                def where(u):
                    hf, i = u // 4, u % 4
                    return hf, i, range(max(0, i - 1) if kind == "A" else 0, i + 1)

                if k == 0:
                    pe.wait_ge(att_ready, a + 1)
                if k < 8:
                    hf, i, ts = where(k)
                    rows = slice(HD * hf, HD * hf + HD)
                    if k >= 2:
                        pe.wait_ge(s_sm, 8 * a + k - 1)
                    mm(ps[:, SC + k % 2, 0:P * len(ts)], q_at[rows, P * i:P * (i + 1)],
                       kk[rows, P * ts[0]:P * (i + 1)], start=True, stop=True).then_inc(s_qk, 1)
                if 1 <= k <= 8:
                    u = k - 1
                    hf, i, ts = where(u)
                    pe.wait_ge(s_nrm, 8 * a + u + 1)
                    if u >= 2:
                        pe.wait_ge(s_pt, 8 * a + u - 1)
                    for j in range(len(ts)):
                        m = nc.tensor.transpose(ps[:, TR + u % 2, P * j:P * (j + 1)], sc[u % 2][:, P * j:P * (j + 1)], ident)
                    m.then_inc(s_tr, 1)
                if k >= 2:
                    u = k - 2
                    hf, i, ts = where(u)
                    cols_ = slice(HD * hf, HD * hf + HD)
                    pe.wait_ge(s_pt, 8 * a + u + 1)
                    for j, t in enumerate(ts):
                        m = mm(ps[cols_, YB, P * i:P * (i + 1)], vv[:, P * t + HD * hf:P * t + HD * hf + HD],
                               pt[u % 2][:, P * j:P * (j + 1)], start=(j == 0), stop=(j == len(ts) - 1))
                    m.then_inc(s_pv, 1)

            def with_steps(kind, G, a, blocks, extra, first, gap):
                plan = [dict() for _ in blocks]
                todo = [(first + gap * k, (lambda k=k: step(kind, G, k, a))) for k in range(10)] + list(extra)
                for pos, work in todo:
                    j = min((pos - 1) // 48, len(blocks) - 1)
                    plan[j].setdefault(pos - 48 * j, []).append(work)
                for (b, s), extras in zip(blocks, plan):
                    proj(b, s, extras)

            def pair_a(i, n0, G):
                n, a = n0 + i, n0 - 1 + i
                b = B_ATT_A + 4 * (n0 - 1) + 4 * i
                with_steps("A", G, a, [(b + j, (1 + j) % 2) for j in range(4)],
                           [(76, lambda: sum_heads(2 + n, [(rope_done, 2 + n)])),
                            (130, lambda: rotate(2 + n, 2 + n, q_st[:, :]))], 12, 18)

            with pe.Fori(0, 4) as i:
                pair_a(i, 1, 0)
            with pe.Fori(0, 3) as i:
                pair_a(i, 5, 1)

            def pair_b(i, n0, kind):
                n, a = n0 + i, n0 - 1 + i
                b = B_ATT_B + 4 * (n0 - 8) + 4 * i
                t = 10 + 2 * (n - 8)
                free = [(rope_done, 10)] if kind == "A" else [(v_sb, 2 + n - 8)]
                with_steps(kind, 1, a, [(b + j, (1 + j) % 2) for j in range(4)],
                           [(76, lambda: sum_heads(t, free)),
                            (124, lambda: sum_heads(t + 1, [(var_ready, t + 1)])),
                            (168, lambda: turn_v(2 + n - 8, b + 2, [(var_ready, t + 2)]))], 12, 18)

            pair_b(0, 8, "A")
            with pe.Fori(0, 7) as i:
                pair_b(i, 9, "B")
            with_steps("B", 0, 15, [(B_EPI + j, (1 + j) % 2) for j in range(3)], [], 12, 13)

            ya, yb = operand(y_hi, y_lo, 0, 8), operand(y_hi, y_lo, 8, 8)

            def branches(i):
                for jj in range(2):
                    for side, (rhs, ready) in enumerate(((ya, 2), (yb, 4))):
                        pe.wait_ge(ylo_ready, ready)
                        stream(B_BRANCH + 4 * i + 2 * jj + side, side,
                               [(4 * jj + 2 * side + ff, (mix_done, 4 * i + 2 * jj - 2), rhs) for ff in range(2)])

            repeat(pe, 4, branches)

            mixed = operand(mix_hi, mix_lo)

            def project_out(i):
                pe.wait_ge(mix_done, CT)
                for f in range(4):
                    t = 4 * i + f
                    stream(B_OUT + t, f % 2, [(MAIN + f % 2, (h_done, t - 1), mixed)])

            repeat(pe, 4, project_out)
            pe.wait_ge(ss2_done, CT)
            mm(ps[:, AUX, :], ones, ss2[:, :], start=True, stop=True).then_inc(ss2_mm, 1)

            hn = operand(hn_hi, hn_lo)
            pe.wait_ge(keys_in, 16)

            def key_scores(t, r):
                pe.wait_ge(qsb_ready, t + 1)
                need(pe, sall, t - 1)
                for i in range(TT):
                    m = mm(ps[:, SC + r, P * i:P * (i + 1)], q_sb[r][:, P * i:P * (i + 1)],
                           keys[:, bass.ds(KEYS * t, KEYS)], start=True, stop=True)
                m.then_inc(ks_mm, 1)

            def queries(i):
                for f in range(4):
                    t = 4 * i + f
                    before = (hlo_ready, 1) if f == 0 else None
                    last = {} if isinstance(t, int) and t == 0 else {24: [lambda t=t, f=f: key_scores(t - 1, (f + 1) % 2)]}
                    stream(B_QUERY + t, f % 2, [(MAIN + f % 2, (qsb_ready, t - 1), hn)], last, before)

            repeat(pe, 4, queries)
            pe.wait_ge(qsb_ready, CT)
            key_scores(CT - 1, 1)

            def down(i, gates=None):
                for e in range(4):
                    t = 4 * i + e
                    extras = {}
                    if gates:
                        extras = {12: [lambda e=e: gates(2 * e)], 36: [lambda e=e: gates(2 * e + 1)]}
                    stream(B_DOWN + t, e % 2, [(MAIN + e % 2, (gel_done, t - 1), hn)], extras)

            repeat(pe, DOWN_TOPK, down)
            pe.wait_ge(tk_done, 1)
            for bank, src in ((TR, tv_all), (TR + 1, i1_all), (YB, i2_all)):
                for i in range(TT):
                    m = nc.tensor.transpose(ps[:, bank, P * i:P * (i + 1)], src[:, P * i:P * (i + 1)], ident)
                m.then_inc(tk_tr, 1)

            def down_and_gates(i):
                g = i - DOWN_TOPK

                def gates(q):
                    n, r = 8 * g + q, q % 2
                    pe.wait_ge(oh_ready, n + 1)
                    need(pe, g_sb, n - 1)
                    for t in range(4):
                        tok = slice(KEYS * t, KEYS * (t + 1))
                        mm(ps[:, SC + r, tok], oh2[r][:, tok], ghi[r][:, tok], start=True, stop=False)
                        m = mm(ps[:, SC + r, tok], oh2[r][:, tok], glo[r][:, tok], start=False, stop=True)
                    m.then_inc(g_mm, 1)

                down(i, gates)

            repeat(pe, DOWN_TOPK + GATE_GROUPS, down_and_gates, DOWN_TOPK)
            with pe.Fori(DOWN_TOPK + GATE_GROUPS, GROUPS) as i:
                down(i)
            pe.wait_ge(gel_done, EXPERT_TILES)

            def up(i):
                for gg in range(2):
                    g = 2 * i + gg
                    rhs = operand(act_hi[gg], act_lo[gg], 0, 4)
                    pe.wait_ge(a_lo, 4 * g + 4)
                    for q in range(4):
                        stream(B_UP + 4 * g + q, q % 2,
                               [((4 * q + d) % 8, (acc_done, CT * g + 4 * q + d - 7), rhs) for d in range(4)])

            repeat(pe, GROUPS // 2, up)


_INS = ["x_t", "w_stream", "small", "keys_t", "rel_ext", "consts"]


def shape_constants():
    c = np.zeros((P, 1920), np.float32)
    p = np.arange(P)
    c[:, 0:128] = np.eye(P)
    c[:, 128:256] = (p[:, None] // HD == p[None, :] // HD)
    rot = HD // 4
    for base in (0, HD):
        for k in range(rot // 2):
            c[base + k + rot // 2, 256 + base + k] = -1.0
            c[base + k, 256 + base + k + rot // 2] = 1.0
    c[:, 384:512] = 1.0
    q, k = p[:, None] // HD, np.arange(256)[None, :] // HD
    c[:, 512:768] = np.where((k == q + 2) | (k == q + 1), 0.0, -1e30)
    c[:, 768:896] = p[None, :]
    inv = (np.float32(500000.0) ** (-np.arange(0, rot, 2, dtype=np.float32) / np.float32(rot))).astype(np.float32)
    ang = np.arange(S, dtype=np.float32)[None, :] * inv[:, None]
    c[:, 896:1408] = 1.0
    for base in (0, HD):
        for part in (0, rot // 2):
            rows = slice(base + part, base + part + rot // 2)
            c[rows, 896:1408] = np.cos(ang)
            c[rows, 1408:1920] = np.sin(ang)
    return c


def lay_out(a):
    x_t = a["x"][0].T.reshape(CT, P, S).transpose(1, 0, 2).reshape(P, CT * S)
    w = np.empty((N_BLOCKS, P, 2048), np.float32)

    def tiles(m):
        return m.reshape(CT, P, -1, P).transpose(2, 1, 0, 3).reshape(-1, P, 2048)

    w_in = tiles(a["w_in"][0])
    qa = a["w_in"][0][:, :A_QW].reshape(D, 2, 2, 4, HD).transpose(0, 1, 3, 2, 4).reshape(D, A_QW)
    qa = tiles(np.ascontiguousarray(qa))
    ka, va, qb = A_QW // P, A_QW // P + 2, A_QW // P + 4
    kb, vb, ga, gb = qb + 8, qb + 16, qb + 24, qb + 24 + CT
    gate = [(ga if g % 2 == 0 else gb) + g // 2 for g in range(N_GATE)]
    order = []
    for n in range(1, 8):
        order += [("q", n)] + gate[3 * (n - 1):3 * n]
    for n in range(8):
        order += [qb + n, kb + n, vb + n, gate[21 + n]]
    order = [ka, ka + 1, va, va + 1, ("q", 0)] + order + gate[29:]
    for b, src in enumerate(order):
        w[b] = qa[src[1]] if isinstance(src, tuple) else w_in[src]
    wa = a["w_branch_a"][0].reshape(2, 2, 4, HD, D).transpose(0, 2, 1, 3, 4).reshape(A_QW, D)
    for side, m in enumerate((wa, a["w_branch_b"][0])):
        w[B_BRANCH + side:B_OUT:2] = m.reshape(8, P, 8, 2, P).transpose(2, 1, 3, 0, 4).reshape(8, P, 2048)
    w[B_OUT:B_QUERY] = tiles(a["w_out"][0])
    w[B_QUERY:B_DOWN] = tiles(a["peer_w_query"][0])
    w[B_DOWN:B_UP] = a["peer_down"][0].reshape(EXPERT_TILES, KEYS, CT, P).transpose(0, 3, 2, 1).reshape(-1, P, 2048)
    up = a["peer_up"][0].reshape(GROUPS, 4, KEYS, 4, 4, P)
    w[B_UP:] = up.transpose(0, 3, 2, 4, 1, 5).reshape(-1, P, 2048)

    small = np.zeros((P, N_COLS), np.float32)
    small[:, C_G1:C_G1 + CT] = a["norm1_gain"][0].reshape(CT, P).T
    small[:, C_G2:C_G2 + CT] = a["norm2_gain"][0].reshape(CT, P).T
    small[:, C_BG:C_BG + N_GATE] = a["b_gate"][0].reshape(2, CT, P).transpose(2, 1, 0).reshape(P, N_GATE)
    for c, name in ((C_QA, "q_norm_a"), (C_KA, "k_norm_a"), (C_QB, "q_norm_b"), (C_KB, "k_norm_b")):
        small[:, c] = np.concatenate([a[name][0], a[name][0]])
    small[:, C_SINK:C_SINK + 16] = a["attn_sinks"][0].reshape(2, 2, 4).transpose(0, 2, 1).reshape(1, 16)
    small[:, C_EPS] = EPS
    keys_t = np.stack([a["peer_sub_keys1"][0], a["peer_sub_keys2"][0]], 1).transpose(3, 0, 1, 2).reshape(P, 16 * KEYS)
    rb = a["rel_bias"][0][:, ::-1]
    ext = np.concatenate([np.repeat(rb[:, :1], 511 - 256, 1), rb, np.repeat(rb[:, -1:], 640 - 255 - rb.shape[1], 1)], 1)
    out = dict(x_t=x_t, w_stream=w, small=small, keys_t=keys_t, rel_ext=ext, consts=shape_constants())
    return {k: np.ascontiguousarray(v) for k, v in out.items()}


def kernel(**inputs):
    import concourse.bacc as bacc
    from concourse.bass_utils import run_bass_kernel_spmd

    arrays = lay_out({k: np.asarray(v) for k, v in inputs.items()})
    nc = bacc.Bacc("TRN2", target_bir_lowering=False, num_devices=1)
    args = [nc.dram_tensor(n, arrays[n].shape, F32, kind="ExternalInput").ap() for n in _INS]
    out = nc.dram_tensor("out", (P, CT * S), F32, kind="ExternalOutput").ap()
    build(nc, *args, out)
    got = run_bass_kernel_spmd(nc, [arrays], core_ids=[0]).results[0]["out"]
    return np.ascontiguousarray(got.reshape(P, CT, S).transpose(2, 1, 0).reshape(1, S, D))
```

```python
import numpy as np
import concourse.bass as bass
from concourse import mybir
from contextlib import ExitStack

D = 2048
S = 512
P = 128
CT = D // P
TT = S // P
HD = 64
EPS = 1e-6
A_PAIRS = 8
B_PAIRS = 8
A_QW, A_KVW, B_W = 1024, 256, 1024
N_GATE = 2 * CT
HEADS = 8
TOPK = 16
KEYS = 128
EXPERT_TILES = 128
GROUPS = EXPERT_TILES // 4

B_PRE = 0
B_ATT_A = 5
B_ATT_B = B_ATT_A + 4 * 7
B_EPI = B_ATT_B + 4 * 8
B_BRANCH = B_EPI + 3
B_OUT = B_BRANCH + 16
B_QUERY = B_OUT + 16
B_DOWN = B_QUERY + 16
B_UP = B_DOWN + EXPERT_TILES
N_BLOCKS = B_UP + 4 * GROUPS

DOWN_TOPK = 11
GATE_GROUPS = 16
GT = S // GATE_GROUPS

MAIN, AUX, SC, TR, YB = 0, 2, 3, 5, 7

F32, F32R, U32 = mybir.dt.float32, mybir.dt.float32r, mybir.dt.uint32
ACT = mybir.ActivationFunctionType
ALU = mybir.AluOpType
AX = mybir.AxisListType.X

C_G1, C_G2, C_BG, C_QA, C_KA, C_QB, C_KB, C_SINK, C_EPS, N_COLS = 0, 16, 32, 64, 65, 66, 67, 68, 84, 85


def need(eng, sem, value):
    if not (isinstance(value, int) and value <= 0):
        eng.wait_ge(sem, value)


def repeat(eng, n, body, first=0):
    body(first)
    if n - first == 2:
        body(first + 1)
    elif n - first > 2:
        with eng.Fori(first + 1, n) as i:
            body(i)


def build(nc, x_t, w_stream, small, keys_t, rel_ext, consts, out):
    ctx = ExitStack()
    with ctx:
        sem = lambda name: ctx.enter_context(nc.semaphore(name))
        K = 1024
        BASE = 16512

        def at(name, kb, cols, dt=F32):
            return nc.alloc_sbuf_tensor_at(name, [P, cols], dt, offset=BASE + int(kb * K))

        raw = [at(f"w_raw{s}", 8 * s, 2048) for s in range(2)]
        whi = [at(f"w_hi{s}", 16 + 8 * s, 2048, F32R) for s in range(2)]
        wlo = [at(f"w_lo{s}", 32 + 8 * s, 2048, F32R) for s in range(2)]
        cst = at("cst", 48, 6 * 128)
        ident, head_ones, rot_t, ones = (cst[:, 128 * k:128 * k + 128] for k in range(4))
        mask_a = at("mask_a", 51, 256)
        iota = at("iota", 52, 128)
        cols = at("cols", 52.5, N_COLS)
        qscaled = at("qscaled", 52.875, 2)
        xn_hi, xn_lo = at("xn_hi", 53, CT * S, F32R), at("xn_lo", 85, CT * S, F32R)
        y_hi, y_lo = at("y_hi", 53, CT * S, F32R), at("y_lo", 85, CT * S, F32R)
        h = at("h", 53, CT * S)
        s_all = at("s_all", 85, TT * 16 * KEYS)
        gate_buf = at("gate_buf", 85, KEYS * GT)
        oh2 = [at(f"oh2_{s}", 101 + 2 * s, 512, F32R) for s in range(2)]
        oh1 = at("oh1", 105, 512)
        g_oh = [at(f"g_oh_{s}", 107 + 4 * s, 1024, F32R) for s in range(2)]
        g_part = [at(f"g_part{s}", kb, 512) for s, kb in enumerate((115, 205))]
        act_hi = [at(f"act_hi{s}", 85 + 8 * s, 4 * S, F32R) for s in range(2)]
        act_lo = [at(f"act_lo{s}", 101 + 8 * s, 4 * S, F32R) for s in range(2)]
        x_raw = at("x_raw", 117, CT * S)
        y_all = at("y_all", 117, CT * S)
        mix_hi, mix_lo = at("mix_hi", 117, CT * S, F32R), at("mix_lo", 149, CT * S, F32R)
        hn_hi, hn_lo = at("hn_hi", 117, CT * S, F32R), at("hn_lo", 149, CT * S, F32R)
        q_st, k_st, q_at, k_at = (at(n, 149 + 2 * k, S) for k, n in enumerate(["q_st", "k_st", "q_at", "k_at"]))
        v_raw, v_st, v_at = (at(n, 157 + 2 * k, S) for k, n in enumerate(["v_raw", "v_st", "v_at"]))
        g_raw = [at(f"g_raw{s}", 163 + 2 * s, S) for s in range(3)]
        sq, var, rst, newt = (at(n, 169 + 2 * k, S) for k, n in enumerate(["sq", "var", "rst", "newt"]))
        cos, sin = at("cos", 177, S), at("sin", 179, S)
        ka = [at(f"ka{g}", 181 + 2 * g, S) for g in range(2)]
        va = [at(f"va{g}", 185 + 2 * g, S) for g in range(2)]
        bias = [at(f"bias{s}", 189 + 2 * s, S) for s in range(2)]
        sc = [at(f"scores{s}", 193 + 2 * s, S) for s in range(2)]
        pt = [at(f"probs_t{s}", 197 + 2 * s, S) for s in range(2)]
        rope_t = at("rope_t", 201, S)
        xn_t = [at(f"xn_t{s}", kb, S) for s, kb in enumerate((197, 199, 203, 205))]
        mx, negm, psm, esk, rcp = (at(n, 207 + k / 32, 2) for k, n in enumerate(["mx", "negm", "psm", "esk", "rcp"]))
        g_in = [at(f"g_in{s}", 181 + 4 * s, 2 * S) for s in range(4)]
        m1 = [at(f"m1_{s}", 197 + 2 * s, S) for s in range(2)]
        m2 = [at(f"m2_{s}", 201 + 2 * s, S) for s in range(2)]
        ss2, sq2, var2, rst2, newt2 = (at(n, 181 + 2 * k, S) for k, n in enumerate(["ss2", "sq2", "var2", "rst2", "newt2"]))
        keys = at("keys", 191, 16 * KEYS)
        q_sb = [at(f"q_sb{s}", 199 + 2 * s, S) for s in range(2)]
        hn_t = [at(f"hn_t{s}", 199 + 2 * s, S) for s in range(4)]
        gel_all = at("gel_all", 181, 4 * S)
        gel = [gel_all[:, S * s:S * (s + 1)] for s in range(4)]
        tk_in, tk_m, cand, cand_m, eq, prod = (
            at(n, 189 + k, 256) for k, n in enumerate(["tk_in", "tk_m", "cand", "cand_m", "eq", "prod"]))
        tk_v, tk_i = at("tk_v", 195, 32), at("tk_i", 195.125, 32, U32)
        tk_if, top_v = at("tk_if", 195.25, 32), at("top_v", 195.375, 16)
        top_p, top_a, top_b = (at(n, 195.5 + k / 16, 16, U32) for k, n in enumerate(["top_p", "top_a", "top_b"]))
        top_f = at("top_f", 195.75, 32)
        i1_all, i2_all, tv_all = (at(n, 196 + 2 * k, S) for k, n in enumerate(["i1_all", "i2_all", "tv_all"]))
        tv_sum, tv_rec = at("tv_sum", 202, 32), at("tv_rec", 202.25, 32)
        i1_t, i2_t = at("i1_t", 189, S), at("i2_t", 191, S)
        gt_hi, gt_lo = at("gt_hi", 193, S), at("gt_lo", 203, S)
        gel_in = [at("gel_in0", 189, 4 * S), at("gel_in1", 117, 4 * S)]
        g_exp = [at("g_exp0", 197, 4 * S), at("g_exp1", 125, 4 * S)]

        ps = ctx.enter_context(nc.psum_tensor("ps", [P, 8, 512], F32))

        bias_skew = nc.dram_tensor("bias_skew", [16, P * 640], F32).ap()
        gate_dram = nc.dram_tensor("gate_dram", [N_GATE, P, S], F32).ap()
        gel_dram = nc.dram_tensor("gel_dram", [GROUPS, P, 4 * S], F32).ap()
        g_dram = nc.dram_tensor("g_dram", [GATE_GROUPS, P, KEYS * GT], F32).ap()

        s_x = [sem(f"x_in{k}") for k in range(4)]
        s_const = sem("consts_in")
        s_ext = sem("rel_ext_spread")
        raw_in = [sem(f"raw_in{s}") for s in range(2)]
        hi_ready, lo_ready = sem("w_hi_ready"), sem("w_lo_ready")
        quarters = sem("mm_quarters")
        sq_acc, xsq, ss_mm = sem("sq_summed"), sem("x_squared"), sem("sum_over_features")
        y0_ready = sem("rsqrt_guess")
        xs_ready, xhi_ready, xlo_ready = sem("x_scaled"), sem("x_hi_ready"), sem("x_lo_ready")
        xlo_pool, hlo_pool = sem("x_lo_odd_tiles"), sem("hn_lo_odd_tiles")
        qs_ready = sem("gains_scaled")
        tile_out = sem("tile_out")
        sq_ready, ss_ready, var_ready, nrm_done = sem("sq_ready"), sem("ss_ready"), sem("var_ready"), sem("nrm_done")
        rot_ready, rope_done = sem("rot_ready"), sem("rope_done")
        vt_ready, v_sb = sem("vt_ready"), sem("v_sb")
        g_out = [sem(f"gate_stored{s}") for s in range(3)]
        att_ready = sem("att_operands")
        s_qk, s_sm, s_exp, s_nrm = sem("scores"), sem("scores_max"), sem("exps"), sem("probs")
        s_tr, s_pt, s_pv, y_done = sem("probs_transposed"), sem("probs_t_sb"), sem("attended"), sem("y_done")
        bias_in = [sem(f"bias_in{s}") for s in range(2)]
        yhi_ready, ylo_ready = sem("y_hi_ready"), sem("y_lo_ready")
        gin = [sem(f"gate_loaded{s}") for s in range(4)]
        gb_ready, sig_ready, mix_done = sem("gate_biased"), sem("gate_sigmoid"), sem("mix_done")
        xh_in, h_done, ss2_done, ss2_mm, y02 = sem("x_again"), sem("h_done"), sem("h_squares"), sem("h_sum"), sem("h_guess")
        hs_ready, hhi_ready, hlo_ready = sem("h_scaled"), sem("hn_hi_ready"), sem("hn_lo_ready")
        keys_in, qsb_ready, ks_mm, sall = sem("keys_in"), sem("query_sb"), sem("key_scores_mm"), sem("key_scores")
        gel_done, gel_out = sem("gelu_done"), sem("gelu_stored")
        tv_sub, tv_exp, tk_done, tk_tr = sem("top_shifted"), sem("top_exp"), sem("topk_done"), sem("topk_transposed")
        gthi_ready, idx_ready = sem("gate_hi_ready"), sem("indices_ready")
        oh_ready, g_mm, gp_ready, g_sb, g_dma = sem("one_hots"), sem("gates_mm"), sem("gates_high_part"), sem("gates_sb"), sem("gates_stored")
        up_in = [sem(f"up_in{s}") for s in range(2)]
        a_mul, a_hi, a_lo = sem("act_product"), sem("act_hi_ready"), sem("act_lo_ready")
        acc_done, s_out = sem("acc_done"), sem("out_stored")

        block = ctx.enter_context(nc.Block())

        def raw_count(base, j, i, per=4):
            return 16 * ((base + j) // 2 + 1) + 8 * per * i

        def skewed(head):
            return bias_skew[head, 127:127 + P * 639].rearrange("(p c) -> p c", c=639)[:, 0:512]

        @block.sync
        def _(sp):
            def load_x(k):
                sp.dma_start(x_raw[:, 2048 * k:2048 * (k + 1)], x_t[:, 2048 * k:2048 * (k + 1)]).then_inc(s_x[k], 16)

            load_x(0)
            load_x(1)
            sp.dma_start(raw[0][:, :], w_stream[0]).then_inc(raw_in[0], 16)
            load_x(2)
            load_x(3)
            sp.dma_start(raw[1][:, :], w_stream[1]).then_inc(raw_in[1], 16)

            def load(i):
                for s in range(2):
                    need(sp, hi_ready, 2 * i + s - 1)
                    need(sp, lo_ready, 2 * i + s - 1)
                    src = w_stream[2 * i + s] if isinstance(i, int) else w_stream[bass.ds(2 * i + s, 1)].rearrange("a p c -> (a p) c")
                    sp.dma_start(raw[s][:, :], src).then_inc(raw_in[s], 16)

            repeat(sp, N_BLOCKS // 2, load, 1)
            for f in range(CT):
                sp.wait_ge(acc_done, CT * (GROUPS - 1) + f + 1)
                sp.dma_start(out[:, S * f:S * (f + 1)], h[:, S * f:S * (f + 1)]).then_inc(s_out, 16)
            sp.wait_ge(s_out, 16 * CT)

        @block.gpsimd
        def _(pool):
            def split(i):
                for s in range(2):
                    pool.wait_ge(hi_ready, 2 * i + s + 1)
                    nc.gpsimd.tensor_tensor(wlo[s][:, :], raw[s][:, :], whi[s][:, :].bitcast(F32),
                                            ALU.subtract).then_inc(lo_ready, 1)

            def low_odd(ring, hi_, lo_, hi_done, done):
                for c in range(1, CT, 2):
                    pool.wait_ge(hi_done, c + 1)
                    nc.gpsimd.tensor_tensor(lo_[:, S * c:S * (c + 1)], ring[c % 4][:, :],
                                            hi_[:, S * c:S * (c + 1)].bitcast(F32), ALU.subtract).then_inc(done, 1)

            split(0)
            low_odd(xn_t, xn_hi, xn_lo, xhi_ready, xlo_pool)
            with pool.Fori(1, B_QUERY // 2 + 1) as i:
                split(i)
            low_odd(hn_t, hn_hi, hn_lo, hhi_ready, hlo_pool)
            with pool.Fori(B_QUERY // 2 + 1, N_BLOCKS // 2) as i:
                split(i)

        @block.scalar
        def _(act):
            def hi(base, j, i=0, per=4):
                s = (base + j) % 2
                b = base + j + per * i
                act.wait_ge(raw_in[s], raw_count(base, j, i, per))
                need(act, quarters, 4 * (b - 1))
                nc.scalar.activation(whi[s][:, :], raw[s][:, :], ACT.Copy).then_inc(hi_ready, 1)

            def take(b, s, dst):
                act.wait_ge(quarters, 4 * b + 4)
                nc.scalar.activation(dst, ps[:, MAIN + s, :], ACT.Copy).then_inc(tile_out, 1)

            def square(b, src):
                act.wait_ge(tile_out, b + 1)
                nc.scalar.activation(sq[:, :], src, ACT.Square).then_inc(sq_ready, 1)

            def rsqrt_guess(t):
                act.wait_ge(ss_ready, t + 1)
                need(act, nrm_done, t)
                nc.scalar.activation(var[:, :], ps[:, AUX, :], ACT.Identity, bias=cols[:, C_EPS:C_EPS + 1],
                                     scale=1.0 / HD)
                act.drain()
                nc.scalar.activation(rst[:, :], var[:, :], ACT.Ln)
                act.drain()
                nc.scalar.activation(rst[:, :], rst[:, :], ACT.Exp, scale=-0.5).then_inc(var_ready, 1)

            def take_v(t, dst):
                act.wait_ge(vt_ready, t + 1)
                nc.scalar.activation(dst, ps[:, AUX, :], ACT.Copy).then_inc(v_sb, 1)

            def take_gate(b, s, slot, gi, stored):
                need(act, g_out[slot], 16 * stored)
                take(b, s, g_raw[slot][:, :])
                act.wait_ge(tile_out, b + 1)
                dst = gate_dram[gi] if isinstance(gi, int) else gate_dram[bass.ds(gi, 1)].rearrange("a p c -> (a p) c")
                act.dma_start(dst, g_raw[slot][:, :]).then_inc(g_out[slot], 16)

            def keys_of(kind, s):
                return min(s % 4 + 1, 2 if kind == "A" else 4)

            def step(kind, k, a):
                if 1 <= k <= 8:
                    u = k - 1
                    n = keys_of(kind, u) * P
                    act.wait_ge(s_tr, 8 * a + u + 1)
                    if u >= 2:
                        act.wait_ge(s_pv, 8 * a + u - 1)
                    nc.scalar.activation(pt[u % 2][:, 0:n], ps[:, TR + u % 2, 0:n], ACT.Copy).then_inc(s_pt, 1)
                if k < 8:
                    n, r = keys_of(kind, k) * P, k % 2
                    act.wait_ge(s_sm, 8 * a + k + 1)
                    e = nc.scalar.activation(sc[r][:, 0:n], sc[r][:, 0:n], ACT.Exp, bias=negm[:, r:r + 1],
                                             accum_out=psm[:, r:r + 1])
                    if kind == "A":
                        c = C_SINK + 2 * a + k // 4
                        e = nc.scalar.activation(esk[:, r:r + 1], cols[:, bass.ds(c, 1)], ACT.Exp, bias=negm[:, r:r + 1])
                    e.then_inc(s_exp, 1)

            def load_bias(head, slot):
                act.dma_start(bias[slot][:, :], skewed(head)).then_inc(bias_in[slot], 16)

            act.dma_start(cst[:, 0:512], consts[:, 0:512]).then_inc(s_const, 16)
            act.dma_start(mask_a[:, :], consts[:, 512:768]).then_inc(s_const, 16)
            act.dma_start(iota[:, :], consts[:, 768:896]).then_inc(s_const, 16)
            act.dma_start(cos[:, :], consts[:, 896:1408]).then_inc(s_const, 16)
            act.dma_start(sin[:, :], consts[:, 1408:1920]).then_inc(s_const, 16)
            act.dma_start(cols[:, :], small).then_inc(s_const, 16)
            for c in range(CT):
                if c % 4 == 0:
                    act.wait_ge(s_x[c // 4], 16)
                if c == 8:
                    hi(B_PRE, 0)
                if c >= 4:
                    act.wait_ge(sq_acc, c - 3)
                nc.scalar.activation(xn_t[c % 4][:, :], x_raw[:, S * c:S * (c + 1)], ACT.Square).then_inc(xsq, 1)
            act.wait_ge(s_const, 96)
            act.wait_ge(ss_mm, 1)
            nc.scalar.activation(var[:, :], ps[:, AUX, :], ACT.Identity, bias=cols[:, C_EPS:C_EPS + 1], scale=1.0 / D)
            act.drain()
            nc.scalar.activation(rst[:, :], var[:, :], ACT.Ln)
            act.drain()
            nc.scalar.activation(rst[:, :], rst[:, :], ACT.Exp, scale=-0.5).then_inc(y0_ready, 1)
            hi(B_PRE, 1)
            for c in range(CT):
                act.wait_ge(xs_ready, c + 1)
                nc.scalar.activation(xn_hi[:, S * c:S * (c + 1)], xn_t[c % 4][:, :], ACT.Copy).then_inc(xhi_ready, 1)
            act.dma_start(bias_skew.rearrange("h (p c) -> h p c", c=640),
                          rel_ext[:, :].rearrange("h (o c) -> h o c", o=1).to_broadcast([16, P, 640])).then_inc(s_ext, 16)

            take(0, 0, k_st[:, :])
            hi(B_PRE, 2)
            square(0, k_st[:, :])
            rsqrt_guess(0)
            take(1, 1, q_at[:, :])
            hi(B_PRE, 3)
            square(1, q_at[:, :])
            rsqrt_guess(1)
            take(2, 0, q_st[:, :])
            hi(B_PRE, 4)
            square(2, q_st[:, :])
            rsqrt_guess(2)
            take(3, 1, v_raw[:, :])
            hi(B_ATT_A, 0)
            take_v(0, va[0][:, :])
            take(4, 0, v_raw[:, :])
            take_v(1, va[1][:, :])

            def pair_a(i, n0):
                n, a = n0 + i, n0 - 1 + i
                b0 = B_ATT_A + 4 * (n0 - 1)
                b = b0 + 4 * i
                if not (isinstance(n, int) and n == 1):
                    take_gate(b - 1, 0, 2, 3 * n - 4, n - 2)
                hi(b0, 1, i)
                step("A", 0, a)
                step("A", 1, a)
                act.wait_ge(att_ready, a + 1)
                take(b, 1, q_st[:, :])
                hi(b0, 2, i)
                square(b, q_st[:, :])
                step("A", 2, a)
                step("A", 3, a)
                rsqrt_guess(2 + n)
                step("A", 4, a)
                take_gate(b + 1, 0, 0, 3 * n - 3, n - 1)
                hi(b0, 3, i)
                for k in (5, 6, 7):
                    step("A", k, a)
                take_gate(b + 2, 1, 1, 3 * n - 2, n - 1)
                hi(b0, 4, i)
                step("A", 8, a)
                step("A", 9, a)

            pair_a(0, 1)
            pair_a(0, 2)
            with act.Fori(0, 5) as i:
                pair_a(i, 3)

            def pair_b(i, n0, kind):
                n, a = n0 + i, n0 - 1 + i
                b0 = B_ATT_B + 4 * (n0 - 8)
                b = b0 + 4 * i
                if kind == "A":
                    take_gate(b - 1, 0, 2, 20, 6)
                else:
                    take_gate(b - 1, 0, 0, 12 + n, n - 2)
                hi(b0, 1, i)
                step(kind, 0, a)
                if kind == "B":
                    load_bias(2 * (a - 8) + 1, 1)
                step(kind, 1, a)
                act.wait_ge(att_ready, a + 1)
                take(b, 1, q_st[:, :])
                hi(b0, 2, i)
                square(b, q_st[:, :])
                step(kind, 2, a)
                step(kind, 3, a)
                rsqrt_guess(10 + 2 * (n - 8))
                step(kind, 4, a)
                take(b + 1, 0, k_st[:, :])
                hi(b0, 3, i)
                square(b + 1, k_st[:, :])
                step(kind, 5, a)
                if kind == "A":
                    act.wait_ge(s_ext, 16)
                load_bias(2 * (a - 7), 0)
                step(kind, 6, a)
                rsqrt_guess(11 + 2 * (n - 8))
                step(kind, 7, a)
                take(b + 2, 1, v_raw[:, :])
                hi(b0, 4, i)
                step(kind, 8, a)
                take_v(2 + n - 8, v_st[:, :])
                step(kind, 9, a)

            pair_b(0, 8, "A")
            with act.Fori(0, 7) as i:
                pair_b(i, 9, "B")

            take_gate(B_EPI - 1, 0, 0, 28, 14)
            hi(B_EPI, 1)
            load_bias(15, 1)
            for k in (0, 1, 2, 3):
                step("B", k, 15)
            take_gate(B_EPI, 1, 0, 29, 15)
            hi(B_EPI, 2)
            for k in (4, 5, 6):
                step("B", k, 15)
            take_gate(B_EPI + 1, 0, 1, 30, 7)
            hi(B_EPI, 3)
            for k in (7, 8, 9):
                step("B", k, 15)

            act.wait_ge(quarters, 4 * B_BRANCH)
            for c in range(CT):
                if c == 1:
                    take_gate(B_EPI + 2, 1, 2, 31, 7)
                if c == 4:
                    hi(B_BRANCH, 1)
                act.wait_ge(y_done, c + 1)
                nc.scalar.activation(y_hi[:, S * c:S * (c + 1)], y_all[:, S * c:S * (c + 1)],
                                     ACT.Copy).then_inc(yhi_ready, 1)
            for slot, count in ((0, 16), (1, 8), (2, 8)):
                act.wait_ge(g_out[slot], 16 * count)

            def branches(i):
                act.wait_ge(ylo_ready, CT)
                need(act, mix_done, 4 * i)
                for f in range(4):
                    act.dma_start(g_in[f][:, :].rearrange("p (g t) -> p g t", g=2),
                                  gate_dram[bass.ds(8 * i + 2 * f, 2)].rearrange("g p t -> p g t")).then_inc(gin[f], 16)
                for f in range(4):
                    hi(B_BRANCH, f + 2, i)
                    act.wait_ge(gb_ready, 4 * i + f + 1)
                    nc.scalar.activation(g_in[f][:, :], g_in[f][:, :], ACT.Sigmoid).then_inc(sig_ready, 1)

            repeat(act, 4, branches)

            act.wait_ge(quarters, 4 * B_OUT)
            act.dma_start(h[:, :], x_t).then_inc(xh_in, 16)
            act.wait_ge(mix_done, 16)
            act.dma_start(keys[:, :], keys_t).then_inc(keys_in, 16)

            def project_out(i):
                for f in range(4):
                    hi(B_OUT, f + 2, i)

            repeat(act, 4, project_out)

            nc.scalar.activation(newt2[:, 0:1], cols[:, C_EPS:C_EPS + 1], ACT.Sqrt)
            act.drain()
            act.wait_ge(ss2_mm, 1)
            nc.scalar.activation(rst2[:, :], ps[:, AUX, :], ACT.Sqrt, bias=cols[:, C_EPS:C_EPS + 1],
                                 scale=1.0 / D).then_inc(y02, 1)
            for c in range(CT):
                act.wait_ge(hs_ready, c + 1)
                nc.scalar.activation(hn_hi[:, S * c:S * (c + 1)], hn_t[c % 4][:, :], ACT.Copy).then_inc(hhi_ready, 1)

            def queries(i):
                for f in range(4):
                    t = 4 * i + f
                    act.wait_ge(quarters, 4 * (B_QUERY + t) + 4)
                    need(act, ks_mm, t - 1)
                    nc.scalar.activation(q_sb[f % 2][:, :], ps[:, MAIN + f % 2, :], ACT.Copy).then_inc(qsb_ready, 1)
                    hi(B_QUERY, f + 2, i)

            repeat(act, 4, queries)

            def gelus(i, extra=None):
                for e in range(4):
                    t = 4 * i + e
                    if extra:
                        extra(2 * e)
                        extra(2 * e + 1)
                    act.wait_ge(quarters, 4 * (B_DOWN + t) + 4)
                    if e == 0:
                        need(act, gel_out, 16 * i)
                    nc.scalar.activation(gel[e], ps[:, MAIN + e % 2, :], ACT.Gelu).then_inc(gel_done, 1)
                    hi(B_DOWN, e + 2, i)
                act.wait_ge(gel_done, 4 * i + 4)
                dst = gel_dram[i] if isinstance(i, int) else gel_dram[bass.ds(i, 1)].rearrange("a p c -> (a p) c")
                act.dma_start(dst, gel_all[:, :]).then_inc(gel_out, 16)

            repeat(act, DOWN_TOPK - 2, gelus)
            act.wait_ge(tv_sub, 1)
            nc.scalar.activation(tv_all[:, :], tv_all[:, :], ACT.Exp).then_inc(tv_exp, 1)
            gelus(DOWN_TOPK - 2)
            act.wait_ge(tk_tr, 1)
            nc.scalar.activation(gt_hi[:, :].bitcast(F32R), ps[:, TR, :], ACT.Copy).then_inc(gthi_ready, 1)
            gelus(DOWN_TOPK - 1)

            def store_gates(g):
                act.wait_ge(g_sb, 8 * g + 8)
                dst = g_dram[g] if isinstance(g, int) else g_dram[bass.ds(g, 1)].rearrange("a p c -> (a p) c")
                act.dma_start(dst, gate_buf[:, :]).then_inc(g_dma, 16)

            def gelus_and_gates(i):
                g = i - DOWN_TOPK


                def high_part(q):
                    if q == 0 and not isinstance(g, int):
                        store_gates(g - 1)
                    act.wait_ge(g_mm, 8 * g + q + 1)
                    need(act, g_sb, 8 * g + q - 1)
                    r = q % 2
                    nc.scalar.activation(
                        g_part[r][:, :].rearrange("p (t k) -> p t k", t=4),
                        ps[:, SC + 2 * r:SC + 2 * r + 2, :].rearrange("p b (t h k) -> p h (b t) k", t=2, h=2)[:, 0],
                        ACT.Copy).then_inc(gp_ready, 1)

                gelus(i, high_part)

            repeat(act, DOWN_TOPK + GATE_GROUPS, gelus_and_gates, DOWN_TOPK)
            store_gates(GATE_GROUPS - 1)

            g_view = g_dram.rearrange("g p (k c) -> p g k c", c=4 * GT)

            def load_group(g, s):
                dst = gel_dram[g] if isinstance(g, int) else gel_dram[bass.ds(g, 1)].rearrange("a p c -> (a p) c")
                act.dma_start(gel_in[s][:, :], dst).then_inc(up_in[s], 16)
                act.dma_start(g_exp[s][:, :].rearrange("p (g c) -> p g c", g=GATE_GROUPS),
                              g_view[:, :, bass.ds(g, 1), :].rearrange("p g k c -> p (g k) c")).then_inc(up_in[s], 16)

            def act_high(n, s, e):
                act.wait_ge(a_mul, n + 1)
                nc.scalar.activation(act_hi[s][:, S * e:S * (e + 1)], gel_in[s][:, S * e:S * (e + 1)],
                                     ACT.Copy).then_inc(a_hi, 1)

            act.wait_ge(g_dma, 16 * GATE_GROUPS)
            act.wait_ge(idx_ready, 2)
            load_group(0, 0)
            with act.Fori(DOWN_TOPK + GATE_GROUPS, GROUPS - 1) as i:
                gelus(i)
            for e in range(4):
                act_high(e, 0, e)
            gelus(GROUPS - 1)
            act.wait_ge(quarters, 4 * B_UP)
            act.wait_ge(gel_out, 16 * GROUPS)
            load_group(1, 1)

            def up(i, last=False):
                for gg in range(2):
                    g = 2 * i + gg
                    if not last:
                        act.wait_ge(a_lo, 4 * g + 4)
                        load_group(g + 2, gg)
                    for q in range(4):
                        if not (last and gg == 1 and q >= 2):
                            hi(B_UP, 4 * gg + q + 2, i, 8)
                        if q == 0 and not (last and gg == 1):
                            for e in range(4):
                                act_high(4 * g + 4 + e, 1 - gg, e)

            up(0)
            with act.Fori(1, GROUPS // 2 - 1) as i:
                up(i)
            up(GROUPS // 2 - 1, last=True)

        @block.vector
        def _(v):
            vec = nc.vector

            def newton(var_, rst_, newt_):
                vec.tensor_tensor(newt_[:, :], rst_[:, :], rst_[:, :], ALU.mult)
                v.drain()
                vec.tensor_tensor(newt_[:, :], newt_[:, :], var_[:, :], ALU.mult)
                v.drain()
                vec.tensor_scalar(newt_[:, :], newt_[:, :], -0.5, 1.5, ALU.mult, ALU.add)
                v.drain()

            def normed(t, dst, gain):
                v.wait_ge(var_ready, t + 1)
                newton(var, rst, newt)
                vec.scalar_tensor_tensor(out=dst, in0=dst, scalar=gain, in1=rst[:, :], op0=ALU.mult, op1=ALU.mult)
                v.drain()
                vec.tensor_tensor(dst, dst, newt[:, :], ALU.mult).then_inc(nrm_done, 1)

            def rope(t, src, dst):
                v.wait_ge(rot_ready, t + 1)
                vec.tensor_tensor(rope_t[:, :], ps[:, AUX, :], sin[:, :], ALU.mult)
                vec.tensor_tensor(dst, src, cos[:, :], ALU.mult)
                v.drain()
                vec.tensor_tensor(dst, dst, rope_t[:, :], ALU.add).then_inc(rope_done, 1)

            for c in range(CT):
                v.wait_ge(xsq, c + 1)
                if c == 0:
                    vec.tensor_copy(sq[:, :], xn_t[0][:, :]).then_inc(sq_acc, 1)
                else:
                    vec.tensor_tensor(sq[:, :], sq[:, :], xn_t[c % 4][:, :], ALU.add).then_inc(sq_acc, 1)
                v.drain()
            v.wait_ge(s_const, 96)
            for k, c in enumerate((C_QA, C_QB)):
                vec.tensor_scalar(qscaled[:, k:k + 1], cols[:, c:c + 1], HD ** -0.5, None, ALU.mult).then_inc(qs_ready, 1)
            v.wait_ge(y0_ready, 1)
            newton(var, rst, newt)
            vec.tensor_tensor(rst[:, :], rst[:, :], newt[:, :], ALU.mult)
            v.drain()

            def normed_tiles(src, gain, rstd, ring, hi_, lo_, scaled, hi_done, lo_done, lo_pool):
                def low(c):
                    v.wait_ge(hi_done, c + 1)
                    vec.tensor_tensor(lo_[:, S * c:S * (c + 1)], ring[c % 4][:, :],
                                      hi_[:, S * c:S * (c + 1)].bitcast(F32), ALU.subtract).then_inc(lo_done, 1)
                for c in range(CT):
                    if c >= 4 and c % 2:
                        v.wait_ge(lo_pool, c // 2 - 1)
                    elif c >= 4:
                        v.drain()
                    vec.scalar_tensor_tensor(out=ring[c % 4][:, :], in0=src[:, S * c:S * (c + 1)],
                                             scalar=cols[:, gain + c:gain + c + 1], in1=rstd[:, :],
                                             op0=ALU.mult, op1=ALU.mult).then_inc(scaled, 1)
                    if c >= 2 and c % 2 == 0:
                        low(c - 2)
                low(CT - 2)

            normed_tiles(x_raw, C_G1, rst, xn_t, xn_hi, xn_lo, xs_ready, xhi_ready, xlo_ready, xlo_pool)

            v.drain()
            normed(0, k_st[:, :], cols[:, C_KA:C_KA + 1])
            rope(0, k_st[:, :], ka[0][:, :])
            normed(1, q_at[:, :], cols[:, C_KA:C_KA + 1])
            rope(1, q_at[:, :], ka[1][:, :])
            normed(2, q_st[:, :], qscaled[:, 0:1])
            rope(2, q_st[:, :], q_st[:, :])

            def step(kind, k, a):
                if k >= 8:
                    return
                n, r = min(k % 4 + 1, 2 if kind == "A" else 4) * P, k % 2
                if k >= 2:
                    v.wait_ge(s_tr, 8 * a + k - 1)
                if kind == "B" and k % 4 == 0:
                    v.wait_ge(bias_in[k // 4], 16 * (a - 7))
                    tail = bias[k // 4][:, 512 - P:512]
                    vec.tensor_tensor(tail, tail, mask_a[:, P:2 * P], ALU.add)
                    v.drain()
                v.wait_ge(s_qk, 8 * a + k + 1)
                b = mask_a[:, 256 - n:256] if kind == "A" else bias[k // 4][:, 512 - n:512]
                vec.tensor_tensor(sc[r][:, 0:n], ps[:, SC + r, 0:n], b, ALU.add)
                v.drain()
                vec.reduce_max(mx[:, r:r + 1], sc[r][:, 0:n], AX)
                v.drain()
                if kind == "A":
                    c = C_SINK + 2 * a + k // 4
                    vec.tensor_scalar(negm[:, r:r + 1], mx[:, r:r + 1], cols[:, bass.ds(c, 1)], -1.0,
                                      ALU.max, ALU.mult).then_inc(s_sm, 1)
                else:
                    vec.tensor_scalar(negm[:, r:r + 1], mx[:, r:r + 1], -1.0, None, ALU.mult).then_inc(s_sm, 1)
                v.wait_ge(s_exp, 8 * a + k + 1)
                if kind == "A":
                    vec.tensor_tensor(psm[:, r:r + 1], psm[:, r:r + 1], esk[:, r:r + 1], ALU.add)
                    v.drain()
                vec.reciprocal(rcp[:, r:r + 1], psm[:, r:r + 1])
                v.drain()
                vec.tensor_scalar(sc[r][:, 0:n], sc[r][:, 0:n], rcp[:, r:r + 1], None, ALU.mult).then_inc(s_nrm, 1)

            def attended(a):
                v.wait_ge(s_pv, 8 * a + 8)
                vec.tensor_scalar(y_all[:, bass.ds(S * a, S)], ps[:, YB, :], 1.0, None, ALU.mult).then_inc(y_done, 1)

            def pair_a(i, n0):
                n, a = n0 + i, n0 - 1 + i
                v.drain()
                vec.tensor_copy(q_at[:, :], q_st[:, :]).then_inc(att_ready, 1)
                for k in range(5):
                    step("A", k, a)
                normed(2 + n, q_st[:, :], qscaled[:, 0:1])
                for k in (5, 6, 7):
                    step("A", k, a)
                rope(2 + n, q_st[:, :], q_st[:, :])
                attended(a)

            with v.Fori(0, 4) as i:
                pair_a(i, 1)
            with v.Fori(0, 3) as i:
                pair_a(i, 5)

            def pair_b(i, n0, kind):
                n, a = n0 + i, n0 - 1 + i
                v.drain()
                if kind == "B":
                    vec.tensor_copy(k_at[:, :], k_st[:, :])
                    v.wait_ge(v_sb, 2 + a - 7)
                    vec.tensor_copy(v_at[:, :], v_st[:, :])
                vec.tensor_copy(q_at[:, :], q_st[:, :]).then_inc(att_ready, 1)
                for k in range(5):
                    step(kind, k, a)
                normed(10 + 2 * (n - 8), q_st[:, :], qscaled[:, 1:2])
                for k in (5, 6, 7):
                    step(kind, k, a)
                v.drain()
                normed(11 + 2 * (n - 8), k_st[:, :], cols[:, C_KB:C_KB + 1])
                attended(a)

            pair_b(0, 8, "A")
            with v.Fori(0, 7) as i:
                pair_b(i, 9, "B")
            v.drain()
            vec.tensor_copy(k_at[:, :], k_st[:, :])
            v.wait_ge(v_sb, 10)
            vec.tensor_copy(v_at[:, :], v_st[:, :])
            vec.tensor_copy(q_at[:, :], q_st[:, :]).then_inc(att_ready, 1)
            for k in range(8):
                step("B", k, 15)
            attended(15)

            v.drain()
            for c in range(CT):
                v.wait_ge(yhi_ready, c + 1)
                vec.tensor_tensor(y_lo[:, S * c:S * (c + 1)], y_all[:, S * c:S * (c + 1)],
                                  y_hi[:, S * c:S * (c + 1)].bitcast(F32), ALU.subtract).then_inc(ylo_ready, 1)
            v.drain()

            def branches(i):
                for f in range(4):
                    v.wait_ge(gin[f], 16 * i + 16)
                    for g in range(2):
                        c = C_BG + 8 * i + 2 * f + g
                        e = vec.tensor_scalar(g_in[f][:, S * g:S * (g + 1)], g_in[f][:, S * g:S * (g + 1)],
                                              cols[:, bass.ds(c, 1)], None, ALU.add)
                    e.then_inc(gb_ready, 1)
                for f in range(4):
                    t = 4 * i + f
                    r = f % 2
                    bank = 4 * (f // 2) + r
                    v.wait_ge(sig_ready, t + 1)
                    v.wait_ge(quarters, 4 * (B_BRANCH + 4 * i + 2 * (f // 2) + 1) + 2 * r + 2)
                    vec.tensor_tensor(m1[r][:, :], ps[:, bank, :], g_in[f][:, 0:S], ALU.mult)
                    vec.tensor_tensor(m2[r][:, :], ps[:, bank + 2, :], g_in[f][:, S:2 * S], ALU.mult)
                    v.drain()
                    vec.tensor_tensor(m1[r][:, :], m1[r][:, :], m2[r][:, :], ALU.add)
                    v.drain()
                    vec.tensor_scalar(mix_hi[:, bass.ds(S * t, S)], m1[r][:, :], 1.0, None, ALU.mult)
                    v.drain()
                    vec.tensor_tensor(mix_lo[:, bass.ds(S * t, S)], m1[r][:, :],
                                      mix_hi[:, bass.ds(S * t, S)].bitcast(F32), ALU.subtract).then_inc(mix_done, 1)
                v.drain()

            repeat(v, 4, branches)

            vec.memset(ss2[:, :], 0.0)
            v.wait_ge(xh_in, 16)

            def project_out(i):
                for f in range(4):
                    t = 4 * i + f
                    hf = h[:, bass.ds(S * t, S)]
                    v.drain()
                    v.wait_ge(quarters, 4 * (B_OUT + t) + 4)
                    vec.tensor_tensor(hf, ps[:, MAIN + f % 2, :], hf, ALU.add).then_inc(h_done, 1)
                    v.drain()
                    vec.tensor_tensor(sq2[:, :], hf, hf, ALU.mult)
                    v.drain()
                    vec.tensor_tensor(ss2[:, :], ss2[:, :], sq2[:, :], ALU.add).then_inc(ss2_done, 1)

            repeat(v, 4, project_out)

            v.wait_ge(y02, 1)
            vec.reciprocal(rst2[:, :], rst2[:, :])
            vec.tensor_scalar(var2[:, :], ps[:, AUX, :], 1.0 / D, EPS, ALU.mult, ALU.add)
            v.drain()
            vec.tensor_tensor(newt2[:, :], var2[:, :], rst2[:, :], ALU.mult)
            v.drain()
            vec.scalar_tensor_tensor(out=newt2[:, :], in0=newt2[:, :], scalar=-0.5, in1=rst2[:, :],
                                     op0=ALU.mult, op1=ALU.mult)
            v.drain()
            vec.scalar_tensor_tensor(out=rst2[:, :], in0=newt2[:, :], scalar=1.5, in1=rst2[:, :],
                                     op0=ALU.add, op1=ALU.mult)
            v.drain()

            normed_tiles(h, C_G2, rst2, hn_t, hn_hi, hn_lo, hs_ready, hhi_ready, hlo_ready, hlo_pool)

            s_view = s_all[:, :].rearrange("p (i c) -> p i c", i=TT)

            def queries(i):
                for f in range(4):
                    t = 4 * i + f
                    v.wait_ge(ks_mm, t + 1)
                    vec.tensor_scalar(s_view[:, :, bass.ds(KEYS * t, KEYS)],
                                      ps[:, SC + f % 2, :].rearrange("p (i c) -> p i c", i=TT), 1.0, None,
                                      ALU.mult).then_inc(sall, 1)

            repeat(v, 4, queries)
            v.drain()

            def top16(src, spare, vals, idx):
                for s_, sp_, v_, i_ in zip(src, spare, vals, idx):
                    vec.max(v_[:, 0:8], s_)
                v.drain()
                for s_, sp_, v_, i_ in zip(src, spare, vals, idx):
                    vec.max_index(i_[:, 0:8], v_[:, 0:8], s_)
                    vec.match_replace(sp_, v_[:, 0:8], s_, -3.0e38)
                v.drain()
                for s_, sp_, v_, i_ in zip(src, spare, vals, idx):
                    vec.max(v_[:, 8:16], sp_)
                v.drain()
                for s_, sp_, v_, i_ in zip(src, spare, vals, idx):
                    vec.max_index(i_[:, 8:16], v_[:, 8:16], sp_)
                v.drain()

            def spread(a, n):
                return a.rearrange("p (k o) -> p k o", o=1).to_broadcast([P, TOPK, n])

            def tiled(a, n):
                return a.rearrange("p (o k) -> p o k", o=1).to_broadcast([P, n, TOPK])

            grid = lambda t: t[:, :].rearrange("p (a b) -> p a b", a=TOPK)
            with v.Fori(0, TT * HEADS) as u:
                vec.tensor_scalar(tk_in[:, :], s_all[:, bass.ds(2 * KEYS * u, 2 * KEYS)], 1.0, None, ALU.mult)
                v.drain()
                top16([tk_in[:, 0:128], tk_in[:, 128:256]], [tk_m[:, 0:128], tk_m[:, 128:256]],
                      [tk_v[:, 0:16], tk_v[:, 16:32]], [tk_i[:, 0:16], tk_i[:, 16:32]])
                vec.tensor_copy(tk_if[:, :], tk_i[:, :])
                vec.tensor_tensor(grid(cand), spread(tk_v[:, 0:16], TOPK), tiled(tk_v[:, 16:32], TOPK), ALU.add)
                v.drain()
                top16([cand[:, :]], [cand_m[:, :]], [top_v[:, :]], [top_p[:, :]])
                vec.tensor_scalar(tv_all[:, bass.ds(TOPK * u, TOPK)], top_v[:, :], 1.0, None, ALU.mult)
                vec.tensor_single_scalar(top_a[:, :], top_p[:, :], 4, ALU.logical_shift_right)
                vec.tensor_single_scalar(top_b[:, :], top_p[:, :], 15, ALU.bitwise_and)
                v.drain()
                vec.tensor_copy(top_f[:, 0:16], top_a[:, :])
                vec.tensor_copy(top_f[:, 16:32], top_b[:, :])
                v.drain()
                for half, dst in ((0, i1_all), (1, i2_all)):
                    r = slice(16 * half, 16 * half + 16)
                    vec.tensor_tensor(grid(eq), spread(top_f[:, r], TOPK), tiled(iota[:, 0:TOPK], TOPK), ALU.is_equal)
                    v.drain()
                    vec.tensor_tensor(grid(prod), grid(eq), tiled(tk_if[:, r], TOPK), ALU.mult)
                    v.drain()
                    vec.reduce_sum(dst[:, bass.ds(TOPK * u, TOPK)], grid(prod), AX)
                v.drain()

            per_head = lambda t: t[:, :].rearrange("p (u k) -> p u k", k=TOPK)
            one_each = lambda t: t[:, :].rearrange("p (u o) -> p u o", o=1).to_broadcast([P, TT * HEADS, TOPK])
            vec.tensor_copy(tv_sum[:, :], per_head(tv_all)[:, :, 0])
            v.drain()
            vec.tensor_tensor(per_head(tv_all), per_head(tv_all), one_each(tv_sum), ALU.subtract).then_inc(tv_sub, 1)
            v.wait_ge(tv_exp, 1)
            vec.reduce_sum(tv_sum[:, :], per_head(tv_all), AX)
            v.drain()
            vec.reciprocal(tv_rec[:, :], tv_sum[:, :])
            v.drain()
            vec.tensor_tensor(per_head(tv_all), per_head(tv_all), one_each(tv_rec), ALU.mult).then_inc(tk_done, 1)
            v.wait_ge(tk_tr, 3)
            vec.tensor_copy(i1_t[:, :], ps[:, TR + 1, :])
            vec.tensor_copy(i2_t[:, :], ps[:, YB, :])
            v.wait_ge(gthi_ready, 1)
            vec.tensor_tensor(gt_lo[:, :], ps[:, TR, :], gt_hi[:, :], ALU.subtract).then_inc(idx_ready, 1)
            v.drain()

            quad = lambda t: t[:, :].rearrange("p (t k) -> p t k", t=4)

            def gates_out(g, q):
                v.wait_ge(gp_ready, 8 * g + q + 1)
                if q == 0:
                    need(v, g_dma, 16 * g)
                r = q % 2
                low_part = ps[:, SC + 2 * r:SC + 2 * r + 2, :].rearrange("p b (t h k) -> p h (b t) k", t=2, h=2)[:, 1]
                vec.tensor_tensor(gate_buf[:, :].rearrange("p (k t) -> p t k", t=GT)[:, 4 * q:4 * q + 4, :],
                                  low_part, quad(g_part[r]), ALU.add).then_inc(g_sb, 1)

            def one_hots(g):
                for q in range(8):
                    n, r = 8 * g + q, q % 2
                    four = lambda t: t[:, bass.ds(4 * n, 4)].rearrange("p (t o) -> p t o", o=1).to_broadcast([P, 4, KEYS])
                    line = iota[:, :].rearrange("p (o k) -> p o k", o=1).to_broadcast([P, 4, KEYS])
                    need(v, g_mm, n - 1)
                    vec.tensor_tensor(quad(oh2[r]), line, four(i2_t), ALU.is_equal)
                    vec.tensor_tensor(quad(oh1), line, four(i1_t), ALU.is_equal)
                    v.drain()
                    both = g_oh[r][:, :].rearrange("p (t h k) -> p h t k", t=4, h=2)
                    vec.tensor_tensor(both[:, 0], quad(oh1), four(gt_hi), ALU.mult)
                    vec.tensor_tensor(both[:, 1], quad(oh1), four(gt_lo), ALU.mult).then_inc(oh_ready, 1)
                    if not (isinstance(g, int) and q < 2):
                        gates_out(g if q >= 2 else g - 1, (q - 2) % 8)
                    v.drain()

            repeat(v, GATE_GROUPS, one_hots)
            gates_out(GATE_GROUPS - 1, 6)
            gates_out(GATE_GROUPS - 1, 7)
            vec.memset(tv_sum[:, :], 0.0).then_inc(idx_ready, 1)

            def product(n, s, e):
                vec.tensor_tensor(gel_in[s][:, S * e:S * (e + 1)].rearrange("p (g t) -> p g t", g=GATE_GROUPS),
                                  gel_in[s][:, S * e:S * (e + 1)].rearrange("p (g t) -> p g t", g=GATE_GROUPS),
                                  g_exp[s][:, :].rearrange("p (g k t) -> p g k t", k=4, t=GT)[:, :, e, :],
                                  ALU.mult).then_inc(a_mul, 1)

            def low(n, s, e):
                v.wait_ge(a_hi, n + 1)
                vec.tensor_tensor(act_lo[s][:, S * e:S * (e + 1)], gel_in[s][:, S * e:S * (e + 1)],
                                  act_hi[s][:, S * e:S * (e + 1)].bitcast(F32), ALU.subtract).then_inc(a_lo, 1)

            v.wait_ge(up_in[0], 32)
            for e in range(4):
                product(e, 0, e)
            for e in range(4):
                low(e, 0, e)

            def up(i, last=False):
                for gg in range(2):
                    g = 2 * i + gg
                    for t in range(CT):
                        tile = CT * g + t
                        more = not (last and gg == 1)
                        if t == 0 and more:
                            v.wait_ge(up_in[1 - gg], 32 * i + 32 if gg == 0 else 32 * i + 64)
                            for e in range(4):
                                product(4 * g + 4 + e, 1 - gg, e)
                        v.wait_ge(quarters, 4 * B_UP + tile + 1)
                        ht = h[:, S * t:S * (t + 1)]
                        vec.tensor_tensor(ht, ps[:, (t + 2) % 8, :], ht, ALU.add).then_inc(acc_done, 1)
                        if t in (5, 7, 9, 11) and more:
                            low(4 * g + 4 + t // 2 - 2, 1 - gg, t // 2 - 2)
                    v.drain()

            up(0)
            with v.Fori(1, GROUPS // 2 - 1) as i:
                up(i)
            up(GROUPS // 2 - 1, last=True)

        @block.tensor
        def _(pe):
            mm = nc.tensor.matmul

            def stream(b, s, tiles, extras=None, before=None):
                pe.wait_ge(lo_ready, b + 1)
                extras = extras or {}
                n = 0
                per = 16 // len(tiles)
                for k, (bank, free, rhs) in enumerate(tiles):
                    if free:
                        need(pe, *free)
                    for c in range(per):
                        if before and k == 0:
                            pe.wait_ge(*before(c))
                        w = slice(P * (per * k + c), P * (per * k + c + 1))
                        hi_, lo_ = rhs[c]
                        for lhs, r in ((whi[s], hi_), (whi[s], lo_), (wlo[s], hi_)):
                            m = mm(ps[:, bank, :], lhs[:, w], r, start=(n % (3 * per) == 0),
                                   stop=(n % (3 * per) == 3 * per - 1))
                            n += 1
                            if n % 12 == 0:
                                m.then_inc(quarters, 1)
                            for work in extras.get(n, ()):
                                work()

            def operand(hi_t, lo_t, c0=0, n=CT):
                return [(hi_t[:, S * c:S * (c + 1)], lo_t[:, S * c:S * (c + 1)]) for c in range(c0, c0 + n)]

            def sum_heads(t, waits=()):
                for w in waits:
                    need(pe, *w)
                pe.wait_ge(sq_ready, t + 1)
                mm(ps[:, AUX, :], head_ones, sq[:, :], start=True, stop=True).then_inc(ss_ready, 1)

            def rotate(t, norm, src):
                pe.wait_ge(nrm_done, norm + 1)
                mm(ps[:, AUX, :], rot_t, src, start=True, stop=True).then_inc(rot_ready, 1)

            def turn_v(t, b, waits=()):
                for w in waits:
                    need(pe, *w)
                pe.wait_ge(tile_out, b + 1)
                for i in range(TT):
                    m = nc.tensor.transpose(ps[:, AUX, P * i:P * (i + 1)], v_raw[:, P * i:P * (i + 1)], ident)
                m.then_inc(vt_ready, 1)

            xn = operand(xn_hi, xn_lo)

            def proj(b, s, extras=None, before=None):
                stream(b, s, [(MAIN + s, (tile_out, b - 1), xn)], extras, before)

            pe.wait_ge(s_const, 96)
            pe.wait_ge(sq_acc, CT)
            mm(ps[:, AUX, :], ones, sq[:, :], start=True, stop=True).then_inc(ss_mm, 1)
            halves = lambda even, odd: lambda c: ((even, odd)[c % 2], c // 2 + 1)
            proj(0, 0, before=halves(xlo_ready, xlo_pool))
            proj(1, 1, {24: [lambda: sum_heads(0)]})
            proj(2, 0, {18: [lambda: rotate(0, 0, k_st[:, :])],
                        36: [lambda: sum_heads(1, [(rope_done, 1)])]})
            proj(3, 1, {24: [lambda: rotate(1, 1, q_at[:, :])],
                        42: [lambda: sum_heads(2, [(rope_done, 2)])]})
            proj(4, 0, {30: [lambda: rotate(2, 2, q_st[:, :])],
                        46: [lambda: turn_v(0, 3, [(rope_done, 3)])]})
            turn_v(1, 4, [(v_sb, 1)])

            def step(kind, G, k, a):
                kk, vv = (ka[G], va[G]) if kind == "A" else (k_at, v_at)

                def where(u):
                    hf, i = u // 4, u % 4
                    return hf, i, range(max(0, i - 1) if kind == "A" else 0, i + 1)

                if k == 0:
                    pe.wait_ge(att_ready, a + 1)
                if k < 8:
                    hf, i, ts = where(k)
                    rows = slice(HD * hf, HD * hf + HD)
                    if k >= 2:
                        pe.wait_ge(s_sm, 8 * a + k - 1)
                    mm(ps[:, SC + k % 2, 0:P * len(ts)], q_at[rows, P * i:P * (i + 1)],
                       kk[rows, P * ts[0]:P * (i + 1)], start=True, stop=True).then_inc(s_qk, 1)
                if 1 <= k <= 8:
                    u = k - 1
                    hf, i, ts = where(u)
                    pe.wait_ge(s_nrm, 8 * a + u + 1)
                    if u >= 2:
                        pe.wait_ge(s_pt, 8 * a + u - 1)
                    for j in range(len(ts)):
                        m = nc.tensor.transpose(ps[:, TR + u % 2, P * j:P * (j + 1)], sc[u % 2][:, P * j:P * (j + 1)], ident)
                    m.then_inc(s_tr, 1)
                if k >= 2:
                    u = k - 2
                    hf, i, ts = where(u)
                    cols_ = slice(HD * hf, HD * hf + HD)
                    pe.wait_ge(s_pt, 8 * a + u + 1)
                    for j, t in enumerate(ts):
                        m = mm(ps[cols_, YB, P * i:P * (i + 1)], vv[:, P * t + HD * hf:P * t + HD * hf + HD],
                               pt[u % 2][:, P * j:P * (j + 1)], start=(j == 0), stop=(j == len(ts) - 1))
                    m.then_inc(s_pv, 1)

            def with_steps(kind, G, a, blocks, extra, first, gap):
                plan = [dict() for _ in blocks]
                todo = [(first + gap * k, (lambda k=k: step(kind, G, k, a))) for k in range(10)] + list(extra)
                for pos, work in todo:
                    j = min((pos - 1) // 48, len(blocks) - 1)
                    plan[j].setdefault(pos - 48 * j, []).append(work)
                for (b, s), extras in zip(blocks, plan):
                    proj(b, s, extras)

            def pair_a(i, n0, G):
                n, a = n0 + i, n0 - 1 + i
                b = B_ATT_A + 4 * (n0 - 1) + 4 * i
                with_steps("A", G, a, [(b + j, (1 + j) % 2) for j in range(4)],
                           [(76, lambda: sum_heads(2 + n, [(v_sb, 2), (rope_done, 2 + n)])),
                            (130, lambda: rotate(2 + n, 2 + n, q_st[:, :]))], 12, 18)

            with pe.Fori(0, 4) as i:
                pair_a(i, 1, 0)
            with pe.Fori(0, 3) as i:
                pair_a(i, 5, 1)

            def pair_b(i, n0, kind):
                n, a = n0 + i, n0 - 1 + i
                b = B_ATT_B + 4 * (n0 - 8) + 4 * i
                t = 10 + 2 * (n - 8)
                free = [(rope_done, 10)] if kind == "A" else [(v_sb, 2 + n - 8)]
                with_steps(kind, 1, a, [(b + j, (1 + j) % 2) for j in range(4)],
                           [(76, lambda: sum_heads(t, free)),
                            (124, lambda: sum_heads(t + 1, [(var_ready, t + 1)])),
                            (168, lambda: turn_v(2 + n - 8, b + 2, [(var_ready, t + 2)]))], 12, 18)

            pair_b(0, 8, "A")
            with pe.Fori(0, 7) as i:
                pair_b(i, 9, "B")
            with_steps("B", 0, 15, [(B_EPI + j, (1 + j) % 2) for j in range(3)], [], 12, 13)

            ya, yb = operand(y_hi, y_lo, 0, 8), operand(y_hi, y_lo, 8, 8)

            def branches(i):
                for jj in range(2):
                    for side, rhs in enumerate((ya, yb)):
                        stream(B_BRANCH + 4 * i + 2 * jj + side, side,
                               [(4 * jj + 2 * side + ff, (mix_done, 4 * i + 2 * jj - 2), rhs) for ff in range(2)],
                               before=(lambda c, side=side: (ylo_ready, 1 + 8 * side + c)) if jj == 0 else None)

            repeat(pe, 4, branches)

            mixed = operand(mix_hi, mix_lo)

            def project_out(i):
                pe.wait_ge(mix_done, CT - 2)
                for f in range(4):
                    t = 4 * i + f
                    stream(B_OUT + t, f % 2, [(MAIN + f % 2, (h_done, t - 1), mixed)],
                           before=(lambda c: (mix_done, c + 1)) if f == 0 else None)

            repeat(pe, 4, project_out)
            pe.wait_ge(ss2_done, CT)
            mm(ps[:, AUX, :], ones, ss2[:, :], start=True, stop=True).then_inc(ss2_mm, 1)

            hn = operand(hn_hi, hn_lo)
            pe.wait_ge(keys_in, 16)

            def key_scores(t, r):
                pe.wait_ge(qsb_ready, t + 1)
                need(pe, sall, t - 1)
                for i in range(TT):
                    m = mm(ps[:, SC + r, P * i:P * (i + 1)], q_sb[r][:, P * i:P * (i + 1)],
                           keys[:, bass.ds(KEYS * t, KEYS)], start=True, stop=True)
                m.then_inc(ks_mm, 1)

            def queries(i):
                for f in range(4):
                    t = 4 * i + f
                    before = halves(hlo_ready, hlo_pool) if f == 0 else None
                    last = {} if isinstance(t, int) and t == 0 else {24: [lambda t=t, f=f: key_scores(t - 1, (f + 1) % 2)]}
                    stream(B_QUERY + t, f % 2, [(MAIN + f % 2, (qsb_ready, t - 1), hn)], last, before)

            repeat(pe, 4, queries)
            pe.wait_ge(qsb_ready, CT)
            key_scores(CT - 1, 1)

            def down(i, gates=None):
                for e in range(4):
                    t = 4 * i + e
                    extras = {}
                    if gates:
                        extras = {12: [lambda e=e: gates(2 * e)], 36: [lambda e=e: gates(2 * e + 1)]}
                    stream(B_DOWN + t, e % 2, [(MAIN + e % 2, (gel_done, t - 1), hn)], extras)

            repeat(pe, DOWN_TOPK - 1, down)
            pe.wait_ge(tk_done, 1)
            for bank, src in ((TR, tv_all), (TR + 1, i1_all), (YB, i2_all)):
                for i in range(TT):
                    m = nc.tensor.transpose(ps[:, bank, P * i:P * (i + 1)], src[:, P * i:P * (i + 1)], ident)
                m.then_inc(tk_tr, 1)
            down(DOWN_TOPK - 1)

            def down_and_gates(i):
                g = i - DOWN_TOPK

                def gates(q):
                    n, r = 8 * g + q, q % 2
                    pe.wait_ge(oh_ready, n + 1)
                    need(pe, g_sb, n - 1)
                    for t in range(4):
                        both = slice(2 * KEYS * (t % 2), 2 * KEYS * (t % 2 + 1))
                        m = mm(ps[:, SC + 2 * r + t // 2, both], oh2[r][:, KEYS * t:KEYS * (t + 1)],
                               g_oh[r][:, 2 * KEYS * t:2 * KEYS * (t + 1)], start=True, stop=True)
                    m.then_inc(g_mm, 1)

                down(i, gates)

            repeat(pe, DOWN_TOPK + GATE_GROUPS, down_and_gates, DOWN_TOPK)
            with pe.Fori(DOWN_TOPK + GATE_GROUPS, GROUPS) as i:
                down(i)
            def up(i):
                for gg in range(2):
                    g = 2 * i + gg
                    rhs = operand(act_hi[gg], act_lo[gg], 0, 4)
                    pe.wait_ge(a_lo, 4 * g + 4)
                    for q in range(4):
                        if q == 1:
                            pe.wait_ge(gel_done, EXPERT_TILES)
                        stream(B_UP + 4 * g + q, q % 2,
                               [((4 * q + d + 2) % 8, (acc_done, CT * g + 4 * q + d - 7), rhs) for d in range(4)])

            repeat(pe, GROUPS // 2, up)


_INS = ["x_t", "w_stream", "small", "keys_t", "rel_ext", "consts"]


def shape_constants():
    c = np.zeros((P, 1920), np.float32)
    p = np.arange(P)
    c[:, 0:128] = np.eye(P)
    c[:, 128:256] = (p[:, None] // HD == p[None, :] // HD)
    rot = HD // 4
    for base in (0, HD):
        for k in range(rot // 2):
            c[base + k + rot // 2, 256 + base + k] = -1.0
            c[base + k, 256 + base + k + rot // 2] = 1.0
    c[:, 384:512] = 1.0
    q, k = p[:, None] // HD, np.arange(256)[None, :] // HD
    c[:, 512:768] = np.where((k == q + 2) | (k == q + 1), 0.0, -1e30)
    c[:, 768:896] = p[None, :]
    inv = (np.float32(500000.0) ** (-np.arange(0, rot, 2, dtype=np.float32) / np.float32(rot))).astype(np.float32)
    ang = np.arange(S, dtype=np.float32)[None, :] * inv[:, None]
    c[:, 896:1408] = 1.0
    for base in (0, HD):
        for part in (0, rot // 2):
            rows = slice(base + part, base + part + rot // 2)
            c[rows, 896:1408] = np.cos(ang)
            c[rows, 1408:1920] = np.sin(ang)
    return c


def lay_out(a):
    x_t = a["x"][0].T.reshape(CT, P, S).transpose(1, 0, 2).reshape(P, CT * S)
    w = np.empty((N_BLOCKS, P, 2048), np.float32)

    def tiles(m):
        return m.reshape(CT, P, -1, P).transpose(2, 1, 0, 3).reshape(-1, P, 2048)

    w_in = tiles(a["w_in"][0])
    qa = a["w_in"][0][:, :A_QW].reshape(D, 2, 2, 4, HD).transpose(0, 1, 3, 2, 4).reshape(D, A_QW)
    qa = tiles(np.ascontiguousarray(qa))
    ka, va, qb = A_QW // P, A_QW // P + 2, A_QW // P + 4
    kb, vb, ga, gb = qb + 8, qb + 16, qb + 24, qb + 24 + CT
    gate = [(ga if g % 2 == 0 else gb) + g // 2 for g in range(N_GATE)]
    order = []
    for n in range(1, 8):
        order += [("q", n)] + gate[3 * (n - 1):3 * n]
    for n in range(8):
        order += [qb + n, kb + n, vb + n, gate[21 + n]]
    order = [ka, ka + 1, ("q", 0), va, va + 1] + order + gate[29:]
    for b, src in enumerate(order):
        w[b] = qa[src[1]] if isinstance(src, tuple) else w_in[src]
    wa = a["w_branch_a"][0].reshape(2, 2, 4, HD, D).transpose(0, 2, 1, 3, 4).reshape(A_QW, D)
    for side, m in enumerate((wa, a["w_branch_b"][0])):
        w[B_BRANCH + side:B_OUT:2] = m.reshape(8, P, 8, 2, P).transpose(2, 1, 3, 0, 4).reshape(8, P, 2048)
    w[B_OUT:B_QUERY] = tiles(a["w_out"][0])
    w[B_QUERY:B_DOWN] = tiles(a["peer_w_query"][0])
    w[B_DOWN:B_UP] = a["peer_down"][0].reshape(EXPERT_TILES, KEYS, CT, P).transpose(0, 3, 2, 1).reshape(-1, P, 2048)
    up = a["peer_up"][0].reshape(GROUPS, 4, KEYS, 4, 4, P)
    w[B_UP:] = up.transpose(0, 3, 2, 4, 1, 5).reshape(-1, P, 2048)

    small = np.zeros((P, N_COLS), np.float32)
    small[:, C_G1:C_G1 + CT] = a["norm1_gain"][0].reshape(CT, P).T
    small[:, C_G2:C_G2 + CT] = a["norm2_gain"][0].reshape(CT, P).T
    small[:, C_BG:C_BG + N_GATE] = a["b_gate"][0].reshape(2, CT, P).transpose(2, 1, 0).reshape(P, N_GATE)
    for c, name in ((C_QA, "q_norm_a"), (C_KA, "k_norm_a"), (C_QB, "q_norm_b"), (C_KB, "k_norm_b")):
        small[:, c] = np.concatenate([a[name][0], a[name][0]])
    small[:, C_SINK:C_SINK + 16] = a["attn_sinks"][0].reshape(2, 2, 4).transpose(0, 2, 1).reshape(1, 16)
    small[:, C_EPS] = EPS
    keys_t = np.stack([a["peer_sub_keys1"][0], a["peer_sub_keys2"][0]], 1).transpose(3, 0, 1, 2).reshape(P, 16 * KEYS)
    rb = a["rel_bias"][0][:, ::-1]
    ext = np.concatenate([np.repeat(rb[:, :1], 511 - 256, 1), rb, np.repeat(rb[:, -1:], 640 - 255 - rb.shape[1], 1)], 1)
    out = dict(x_t=x_t, w_stream=w, small=small, keys_t=keys_t, rel_ext=ext, consts=shape_constants())
    return {k: np.ascontiguousarray(v) for k, v in out.items()}


def kernel(**inputs):
    import concourse.bacc as bacc
    from concourse.bass_utils import run_bass_kernel_spmd

    arrays = lay_out({k: np.asarray(v) for k, v in inputs.items()})
    nc = bacc.Bacc("TRN2", target_bir_lowering=False, num_devices=1)
    args = [nc.dram_tensor(n, arrays[n].shape, F32, kind="ExternalInput").ap() for n in _INS]
    out = nc.dram_tensor("out", (P, CT * S), F32, kind="ExternalOutput").ap()
    build(nc, *args, out)
    got = run_bass_kernel_spmd(nc, [arrays], core_ids=[0]).results[0]["out"]
    return np.ascontiguousarray(got.reshape(P, CT, S).transpose(2, 1, 0).reshape(1, S, D))
```
